# Optimizing a Trainium2 kernel written in Bass

```python
import math
import jax
import jax.numpy as jnp
from jax import lax
import numpy as np

D_MODEL = 1024
BATCH = 1
SEQ = 1024
DEPTH = 2

GRID_W = 64
CTX_LEN = 256
F32 = jnp.float32
ALPHA = (2.0 * DEPTH) ** 0.25
BETA = (8.0 * DEPTH) ** -0.25
LN_EPS = 1e-5
NORM_EPS = 1e-6
NEG = -1e30
GLA_HEADS = 4
GLA_DK = 64
GLA_DV = 128
GLA_RANK = 16
GLA_TAU = 16.0
GLA_CHUNK = 64
NA_HEADS = 8
NA_DH = 64
NA_KH = 8
NA_KW = 16
ML_HEADS = 4
ML_DQK = 64
ML_DV = 128
ML_CHUNK = 64
SW_HEADS = 8
SW_KV_HEADS = 2
SW_DH = 64
SW_WINDOW = 128
SW_BLOCK = 128
ROPE_BASE = 10000.0

GLA_W = GLA_HEADS * GLA_DV
NA_W = NA_HEADS * NA_DH
ML_W = ML_HEADS * ML_DV
SW_W = SW_HEADS * SW_DH
EVEN_SPLITS = (GLA_HEADS * GLA_DK, GLA_HEADS * GLA_DK, GLA_W, GLA_W, 2 * GLA_RANK, NA_W, NA_W, NA_W, NA_W)
ODD_SPLITS = (ML_HEADS * ML_DQK, ML_HEADS * ML_DQK, ML_W, ML_W, 4 * ML_HEADS, SW_W, SW_KV_HEADS * SW_DH, SW_KV_HEADS * SW_DH, SW_W)
EVEN_IN = sum(EVEN_SPLITS)
ODD_IN = sum(ODD_SPLITS)
EVEN_OUT = GLA_W + NA_W
ODD_OUT = ML_W + SW_W
N_EVEN = (DEPTH + 1) // 2
N_ODD = DEPTH // 2

kernel_name = 'hybrid_gla_natten_mlstm_swa_block'

def split_cols(a, sizes):
    idx = [int(i) for i in np.cumsum(sizes)[:-1]]
    return jnp.split(a, idx, axis=-1)

def heads(a, h):
    b, t, _ = a.shape
    return a.reshape(b, t, h, -1).transpose(0, 2, 1, 3)

def merge(a):
    b, h, t, d = a.shape
    return a.transpose(0, 2, 1, 3).reshape(b, t, h * d)

def layer_norm(x, g, b):
    xf = x.astype(F32)
    mu = jnp.mean(xf, axis=-1, keepdims=True)
    var = jnp.mean(jnp.square(xf - mu), axis=-1, keepdims=True)
    return ((xf - mu) * lax.rsqrt(var + LN_EPS)).astype(x.dtype) * g + b

def head_rmsnorm(o, g):
    of = o.astype(F32)
    of = of * lax.rsqrt(jnp.mean(jnp.square(of), axis=-1, keepdims=True) + NORM_EPS)
    return merge(of.astype(o.dtype)) * g

def to_chunks(a, c):
    s = a.shape
    return jnp.moveaxis(a.reshape(s[:2] + (s[2] // c, c) + s[3:]), 2, 0)

def from_chunks(a):
    a = jnp.moveaxis(a, 0, 2)
    s = a.shape
    return a.reshape(s[:2] + (s[2] * s[3],) + s[4:])

def flip_t(args):
    return tuple(jnp.flip(a, axis=2) for a in args)

def prefix_scan(scan_fn, lat, ctx, state0):
    o_ctx, st = scan_fn(*ctx, state0)
    o_lat, _ = scan_fn(*lat, st)
    return o_lat, o_ctx

def bidir_prefix(scan_fn, lat_f, ctx_f, lat_b, ctx_b, state0):
    lf, cf = prefix_scan(scan_fn, lat_f, ctx_f, state0)
    lb, cb = prefix_scan(scan_fn, flip_t(lat_b), flip_t(ctx_b), state0)
    return lf + jnp.flip(lb, axis=2), cf + jnp.flip(cb, axis=2)

def gla_scan(q, k, v, g, s0):
    out_dtype = v.dtype
    qs, ks, vs, gs = [to_chunks(a.astype(F32), GLA_CHUNK) for a in (q, k, v, g)]
    tril = jnp.tril(jnp.ones((GLA_CHUNK, GLA_CHUNK), bool))

    def body(S, inp):
        qc, kc, vc, gc = inp
        b = jnp.cumsum(gc, axis=2)
        b_last = b[:, :, -1:, :]
        q_in = qc * jnp.exp(b)
        k_in = kc * jnp.exp(-b)
        a = jnp.where(tril, jnp.einsum('bhtd,bhsd->bhts', q_in, k_in), 0.0)
        o = jnp.einsum('bhts,bhsv->bhtv', a, vc) + jnp.einsum('bhtd,bhdv->bhtv', q_in, S)
        S = jnp.exp(b_last)[:, :, 0, :, None] * S + jnp.einsum('bhsd,bhsv->bhdv', kc * jnp.exp(b_last - b), vc)
        return S, o

    S, o = lax.scan(body, s0, (qs, ks, vs, gs))
    return from_chunks(o).astype(out_dtype), S

def mlstm_scan(q, k, v, ig, lf, state):
    out_dtype = v.dtype
    qs, ks, vs, is_, fs = [to_chunks(a.astype(F32), ML_CHUNK) for a in (q, k, v, ig, lf)]
    tril = jnp.tril(jnp.ones((ML_CHUNK, ML_CHUNK), bool))

    def body(st, inp):
        cm, n, m = st
        qc, kc, vc, ic, fc = inp
        b = jnp.cumsum(fc, axis=-1)
        dmat = jnp.where(tril, b[..., :, None] - b[..., None, :] + ic[..., None, :], NEG)
        inter = b + m[..., None]
        m_t = jnp.maximum(jnp.max(dmat, axis=-1), inter)
        w = jnp.exp(dmat - m_t[..., None])
        w_int = jnp.exp(inter - m_t)
        s = jnp.einsum('bhtd,bhsd->bhts', qc, kc) * w
        num = s @ vc + w_int[..., None] * jnp.einsum('bhtd,bhdv->bhtv', qc, cm)
        den = jnp.sum(s, axis=-1) + w_int * jnp.einsum('bhtd,bhd->bht', qc, n)
        h = num / jnp.maximum(jnp.abs(den), jnp.exp(-m_t))[..., None]
        b_last = b[..., -1]
        ws_log = b_last[..., None] - b + ic
        m_new = jnp.maximum(b_last + m, jnp.max(ws_log, axis=-1))
        dec = jnp.exp(b_last + m - m_new)
        ws = jnp.exp(ws_log - m_new[..., None])
        cm = dec[..., None, None] * cm + jnp.einsum('bhs,bhsd,bhsv->bhdv', ws, kc, vc)
        n = dec[..., None] * n + jnp.einsum('bhs,bhsd->bhd', ws, kc)
        return (cm, n, m_new), h

    st, h = lax.scan(body, state, (qs, ks, vs, is_, fs))
    return from_chunks(h).astype(out_dtype), st

def axial_rope(x, rows, cols):
    half = x.shape[-1] // 2
    nf = half // 2
    freqs = ROPE_BASE ** (-jnp.arange(nf, dtype=F32) / nf)

    def rot(xp, pos):
        ang = pos[:, None] * freqs[None, :]
        cos = jnp.cos(ang).astype(x.dtype)
        sin = jnp.sin(ang).astype(x.dtype)
        x1, x2 = xp[..., :nf], xp[..., nf:]
        return jnp.concatenate([x1 * cos - x2 * sin, x1 * sin + x2 * cos], axis=-1)

    return jnp.concatenate([rot(x[..., :half], rows), rot(x[..., half:], cols)], axis=-1)

def dense_attn(q, k, v, sink=None):
    scale = q.shape[-1] ** -0.5
    s = jnp.einsum('bkgld,bksd->bkgls', q, k).astype(F32) * scale
    if sink is None:
        p = jax.nn.softmax(s, axis=-1)
    else:
        s_sink = jnp.broadcast_to(sink.astype(F32)[None, :, :, None, None], s.shape[:-1] + (1,))
        p = jax.nn.softmax(jnp.concatenate([s, s_sink], axis=-1), axis=-1)[..., :-1]
    return jnp.einsum('bkgls,bksd->bkgld', p.astype(v.dtype), v)

def neighbourhood_attn(q, k, v, kc, vc, rpb):
    b, h, t, dh = q.shape
    rows_n = t // GRID_W
    kh = min(NA_KH, rows_n)
    qg, kg, vg = [a.reshape(b, h, rows_n, GRID_W, dh) for a in (q, k, v)]
    cols = jnp.arange(GRID_W)
    cs = jnp.clip(cols - NA_KW // 2, 0, GRID_W - NA_KW)
    col_ok = (cols[None, :] >= cs[:, None]) & (cols[None, :] < cs[:, None] + NA_KW)
    dc_idx = jnp.clip(cols[None, :] - cols[:, None] + NA_KW - 1, 0, 2 * NA_KW - 2)
    scale = dh ** -0.5
    n_lat = kh * GRID_W

    def row(r):
        rs = jnp.clip(r - kh // 2, 0, rows_n - kh)
        q_r = lax.dynamic_index_in_dim(qg, r, axis=2, keepdims=False)
        k_blk = lax.dynamic_slice_in_dim(kg, rs, kh, axis=2)
        v_blk = lax.dynamic_slice_in_dim(vg, rs, kh, axis=2)
        dr_idx = rs + jnp.arange(kh) - r + NA_KH - 1
        bias = rpb[:, dr_idx[:, None, None], dc_idx[None, :, :]].transpose(0, 2, 1, 3)
        s_lat = jnp.einsum('bhqd,bhiwd->bhqiw', q_r, k_blk).astype(F32) * scale + bias.astype(F32)[None]
        s_lat = jnp.where(col_ok[:, None, :], s_lat, NEG).reshape(b, h, GRID_W, n_lat)
        s_ctx = jnp.einsum('bhqd,bhcd->bhqc', q_r, kc).astype(F32) * scale
        p = jax.nn.softmax(jnp.concatenate([s_lat, s_ctx], axis=-1), axis=-1)
        p_lat = p[..., :n_lat].reshape(b, h, GRID_W, kh, GRID_W).astype(v.dtype)
        p_ctx = p[..., n_lat:].astype(v.dtype)
        return jnp.einsum('bhqiw,bhiwd->bhqd', p_lat, v_blk) + jnp.einsum('bhqc,bhcd->bhqd', p_ctx, vc)

    o = lax.map(row, jnp.arange(rows_n))
    return jnp.moveaxis(o, 0, 2).reshape(b, h, t, dh)

def swa_attn(q, k, v, kc, vc, sink):
    b, h, t, dh = q.shape
    kv = k.shape[1]
    g = h // kv
    n_ctx = kc.shape[2]
    qg = q.reshape(b, kv, g, t, dh)
    nb = t // SW_BLOCK
    span = SW_BLOCK + 2 * SW_WINDOW
    pad = ((0, 0), (0, 0), (SW_WINDOW, SW_WINDOW), (0, 0))
    k_pad = jnp.pad(k, pad)
    v_pad = jnp.pad(v, pad)
    sink_f = sink.reshape(kv, g).astype(F32)
    scale = dh ** -0.5

    def block(n):
        start = n * SW_BLOCK
        q_b = lax.dynamic_slice_in_dim(qg, start, SW_BLOCK, axis=3)
        k_w = lax.dynamic_slice_in_dim(k_pad, start, span, axis=2)
        v_w = lax.dynamic_slice_in_dim(v_pad, start, span, axis=2)
        qpos = start + jnp.arange(SW_BLOCK)
        kpos = start - SW_WINDOW + jnp.arange(span)
        ok = (jnp.abs(qpos[:, None] - kpos[None, :]) <= SW_WINDOW) & (kpos[None, :] >= 0) & (kpos[None, :] < t)
        s_lat = jnp.where(ok, jnp.einsum('bkgqd,bksd->bkgqs', q_b, k_w).astype(F32) * scale, NEG)
        s_ctx = jnp.einsum('bkgqd,bkcd->bkgqc', q_b, kc).astype(F32) * scale
        s_sink = jnp.broadcast_to(sink_f[None, :, :, None, None], s_ctx.shape[:-1] + (1,))
        p = jax.nn.softmax(jnp.concatenate([s_lat, s_ctx, s_sink], axis=-1), axis=-1).astype(v.dtype)
        return (jnp.einsum('bkgqs,bksd->bkgqd', p[..., :span], v_w)
                + jnp.einsum('bkgqc,bkcd->bkgqd', p[..., span:span + n_ctx], vc))

    o = lax.map(block, jnp.arange(nb))
    return jnp.moveaxis(o, 0, 3).reshape(b, h, t, dh)

def mixer_even(h, hc, w_in, w_out, gla_gate_w, gla_gate_b, gla_norm_g, na_rpb, need_ctx):
    pl = split_cols(h @ w_in, EVEN_SPLITS)
    pc = split_cols(hc @ w_in, EVEN_SPLITS)
    bsz = h.shape[0]

    def gla_inputs(parts):
        qa, ka, va, _, lra = parts[:5]
        q = heads(qa, GLA_HEADS) * (GLA_DK ** -0.5)
        k = heads(ka, GLA_HEADS)
        v = heads(va, GLA_HEADS)
        lr = lra.reshape(lra.shape[:-1] + (2, GLA_RANK))
        z = jnp.einsum('btdr,drk->btdk', lr, gla_gate_w) + gla_gate_b
        g = jax.nn.log_sigmoid(z.astype(F32)) / GLA_TAU
        return (q, k, v, heads(g[:, :, 0], GLA_HEADS)), (q, k, v, heads(g[:, :, 1], GLA_HEADS))

    lat_f, lat_b = gla_inputs(pl)
    ctx_f, ctx_b = gla_inputs(pc)
    s0 = jnp.zeros((bsz, GLA_HEADS, GLA_DK, GLA_DV), F32)
    oa_lat, oa_ctx = bidir_prefix(gla_scan, lat_f, ctx_f, lat_b, ctx_b, s0)
    ya = head_rmsnorm(oa_lat, gla_norm_g) * jax.nn.silu(pl[3])

    kbc = heads(pc[6], NA_HEADS)
    vbc = heads(pc[7], NA_HEADS)
    ob = neighbourhood_attn(heads(pl[5], NA_HEADS), heads(pl[6], NA_HEADS), heads(pl[7], NA_HEADS), kbc, vbc, na_rpb)
    yb = merge(ob) * jax.nn.silu(pl[8])
    y_lat = jnp.concatenate([ya, yb], axis=-1) @ w_out
    if not need_ctx:
        return y_lat, None
    ya_c = head_rmsnorm(oa_ctx, gla_norm_g) * jax.nn.silu(pc[3])
    ob_c = dense_attn(heads(pc[5], NA_HEADS)[:, :, None], kbc, vbc)[:, :, 0]
    yb_c = merge(ob_c) * jax.nn.silu(pc[8])
    y_ctx = jnp.concatenate([ya_c, yb_c], axis=-1) @ w_out
    return y_lat, y_ctx

def mixer_odd(h, hc, w_in, w_out, ml_gate_b, ml_norm_g, sw_sink, need_ctx):
    pl = split_cols(h @ w_in, ODD_SPLITS)
    pc = split_cols(hc @ w_in, ODD_SPLITS)
    bsz, t, _ = h.shape

    def mlstm_inputs(parts):
        qm, km, vm, _, gates = parts[:5]
        q = heads(qm, ML_HEADS)
        k = heads(km, ML_HEADS) * (ML_DQK ** -0.5)
        v = heads(vm, ML_HEADS)
        gp = gates.reshape(gates.shape[:2] + (2, 2, ML_HEADS)).astype(F32) + ml_gate_b.astype(F32)
        gp = gp.transpose(2, 3, 0, 4, 1)
        return ((q, k, v, gp[0, 0], jax.nn.log_sigmoid(gp[0, 1])),
                (q, k, v, gp[1, 0], jax.nn.log_sigmoid(gp[1, 1])))

    lat_f, lat_b = mlstm_inputs(pl)
    ctx_f, ctx_b = mlstm_inputs(pc)
    st0 = (jnp.zeros((bsz, ML_HEADS, ML_DQK, ML_DV), F32), jnp.zeros((bsz, ML_HEADS, ML_DQK), F32),
           jnp.zeros((bsz, ML_HEADS), F32))
    oc_lat, oc_ctx = bidir_prefix(mlstm_scan, lat_f, ctx_f, lat_b, ctx_b, st0)
    yc = head_rmsnorm(oc_lat, ml_norm_g) * jax.nn.silu(pl[3])

    pos = jnp.arange(t)
    rows = (pos // GRID_W).astype(F32)
    cols = (pos % GRID_W).astype(F32)
    qd = axial_rope(heads(pl[5], SW_HEADS), rows, cols)
    kd = axial_rope(heads(pl[6], SW_KV_HEADS), rows, cols)
    vd = heads(pl[7], SW_KV_HEADS)
    kdc = heads(pc[6], SW_KV_HEADS)
    vdc = heads(pc[7], SW_KV_HEADS)
    od = swa_attn(qd, kd, vd, kdc, vdc, sw_sink)
    yd = merge(od) * jax.nn.silu(pl[8])
    y_lat = jnp.concatenate([yc, yd], axis=-1) @ w_out
    if not need_ctx:
        return y_lat, None
    yc_c = head_rmsnorm(oc_ctx, ml_norm_g) * jax.nn.silu(pc[3])
    n_ctx = hc.shape[1]
    qdc = heads(pc[5], SW_HEADS).reshape(bsz, SW_KV_HEADS, SW_HEADS // SW_KV_HEADS, n_ctx, SW_DH)
    od_c = dense_attn(qdc, kdc, vdc, sw_sink.reshape(SW_KV_HEADS, SW_HEADS // SW_KV_HEADS))
    yd_c = merge(od_c.reshape(bsz, SW_HEADS, n_ctx, SW_DH)) * jax.nn.silu(pc[8])
    y_ctx = jnp.concatenate([yc_c, yd_c], axis=-1) @ w_out
    return y_lat, y_ctx

def setup_inputs(seed: int = 0) -> dict:
    key = jax.random.key(seed)
    ks = jax.random.split(key, 20)

    def nrm(k, shape, scale):
        return jax.random.normal(k, shape, F32) * scale

    ml_base = jnp.stack([jnp.full((ML_HEADS,), -1.0, F32), jnp.linspace(3.0, 6.0, ML_HEADS, dtype=F32)])
    return {
        'x': nrm(ks[0], (BATCH, SEQ, D_MODEL), 1.0),
        'c': nrm(ks[1], (BATCH, D_MODEL), 1.0),
        'ctx': nrm(ks[2], (BATCH, CTX_LEN, D_MODEL), 1.0),
        'c_ctx': nrm(ks[3], (D_MODEL,), 1.0),
        'w_ada': nrm(ks[4], (DEPTH, D_MODEL, 3 * D_MODEL), 0.5 * D_MODEL ** -0.5),
        'b_ada': nrm(ks[5], (DEPTH, 3 * D_MODEL), 0.02),
        'ln_g': 1.0 + nrm(ks[6], (DEPTH, D_MODEL), 0.02),
        'ln_b': nrm(ks[7], (DEPTH, D_MODEL), 0.02),
        'w_in_even': nrm(ks[8], (N_EVEN, D_MODEL, EVEN_IN), D_MODEL ** -0.5),
        'w_out_even': nrm(ks[9], (N_EVEN, EVEN_OUT, D_MODEL), BETA * EVEN_OUT ** -0.5),
        'gla_gate_w': nrm(ks[10], (N_EVEN, 2, GLA_RANK, GLA_HEADS * GLA_DK), GLA_RANK ** -0.5),
        'gla_gate_b': 2.0 + nrm(ks[11], (N_EVEN, 2, GLA_HEADS * GLA_DK), 0.1),
        'gla_norm_g': 1.0 + nrm(ks[12], (N_EVEN, GLA_W), 0.02),
        'na_rpb': nrm(ks[13], (N_EVEN, NA_HEADS, 2 * NA_KH - 1, 2 * NA_KW - 1), 0.1),
        'w_in_odd': nrm(ks[14], (N_ODD, D_MODEL, ODD_IN), D_MODEL ** -0.5),
        'w_out_odd': nrm(ks[15], (N_ODD, ODD_OUT, D_MODEL), BETA * ODD_OUT ** -0.5),
        'ml_gate_b': ml_base[None, None] + nrm(ks[16], (N_ODD, 2, 2, ML_HEADS), 0.1),
        'ml_norm_g': 1.0 + nrm(ks[17], (N_ODD, ML_W), 0.02),
        'sw_sink': nrm(ks[18], (N_ODD, SW_HEADS), 0.5),
    }

def reference(x, c, ctx, c_ctx, w_ada, b_ada, ln_g, ln_b, w_in_even, w_out_even, gla_gate_w, gla_gate_b,
              gla_norm_g, na_rpb, w_in_odd, w_out_odd, ml_gate_b, ml_norm_g, sw_sink):
    cond = jax.nn.silu(c)
    cond_ctx = jax.nn.silu(c_ctx)
    cx = ctx
    for l in range(DEPTH):
        need_ctx = l < DEPTH - 1
        shift, scale, gate = jnp.split(cond @ w_ada[l] + b_ada[l], 3, axis=-1)
        shift_c, scale_c, gate_c = jnp.split(cond_ctx @ w_ada[l] + b_ada[l], 3, axis=-1)
        h = x * (1.0 + scale[:, None]) + shift[:, None]
        hc = cx * (1.0 + scale_c) + shift_c
        i = l // 2
        if l % 2 == 0:
            y, yc = mixer_even(h, hc, w_in_even[i], w_out_even[i], gla_gate_w[i], gla_gate_b[i],
                               gla_norm_g[i], na_rpb[i], need_ctx)
        else:
            y, yc = mixer_odd(h, hc, w_in_odd[i], w_out_odd[i], ml_gate_b[i], ml_norm_g[i], sw_sink[i], need_ctx)
        x = layer_norm(ALPHA * x + gate[:, None] * y, ln_g[l], ln_b[l])
        if need_ctx:
            cx = layer_norm(ALPHA * cx + gate_c * yc, ln_g[l], ln_b[l])
    return x


_drawn_inputs = setup_inputs


def setup_inputs(seed=0):
    import zlib

    import numpy as np

    out = dict(_drawn_inputs(seed))
    spreads = {}
    factors = {'ctx': 3.936,
     'c_ctx': 3.433,
     'b_ada': 6.716,
     'gla_gate_w': 4.282,
     'gla_gate_b': 8.0,
     'gla_norm_g': 38.57,
     'na_rpb': 64.0,
     'ml_norm_g': 60.042,
     'sw_sink': 64.0}
    for name, (base, spread) in spreads.items():
        noise = np.random.default_rng([zlib.crc32(name.encode()), seed]).standard_normal(out[name].shape)
        drawn = base * np.exp(spread * noise) if base else spread * noise
        out[name] = jnp.asarray(drawn.astype(out[name].dtype))
    for name, factor in factors.items():
        out[name] = (out[name] * factor).astype(out[name].dtype)
    return out
```

```python
from contextlib import ExitStack

import numpy as np

import concourse.bass as bass
from concourse import mybir

ALU = mybir.AluOpType
ACT = mybir.ActivationFunctionType
AX_X = mybir.AxisListType.X
F32 = mybir.dt.float32

P = 128
D = 1024
KT = D // P
LAT = 1024
CTX = 256
T = CTX + LAT
NT = T // P
CT = CTX // P
DEPTH = 2
ALPHA = (2.0 * DEPTH) ** 0.25
LN_EPS = 1e-5
RMS_EPS = 1e-6
GLA_TAU = 16.0
CHUNK = 64
GRID_W = 64
ROWS = LAT // GRID_W
DH = 64
QSCALE = DH ** -0.5
NEG = -1e30
LOWEST = -3.0e38
FULL_BIAS = 14 * GRID_W
MID_BIAS = 9 * GRID_W
BIAS = FULL_BIAS + MID_BIAS
VW = 129
GATE_ROWS = 64
WBUFS = 5

CHUNKS_ALL = [(0, CTX), (CTX, 512), (CTX + 512, 512)]
CHUNKS_LAT = CHUNKS_ALL[1:]

CONST = {}
_off = 0
for _name, _w in (("ident", P), ("tri_f", P), ("tri_b", P), ("stri_f", P), ("stri_b", P), ("ones", P),
                  ("mask", 2 * P), ("add", 2 * P), ("perm", P), ("band", 3 * P)):
    CONST[_name] = (_off, _w)
    _off += _w
CONST_W = _off
SEL_AT = 2 * LAT
TABLES_W = SEL_AT + 12 * P
COLS = {}
_off = 0
for _name, _w in (("b_ada", 2 * 24), ("ln_g", 2 * KT), ("ln_b", 2 * KT), ("norm_g", 2 * 4), ("sink", 8), ("gate_b", 1),
                  ("cond", 16), ("eps", 2), ("one", 1)):
    COLS[_name] = (_off, _w)
    _off += _w
COLS_W = _off


def units_even(j):
    out = []
    for t in range(2, NT):
        r = 2 * (t - CT)
        rs = min(max(r - 4, 0), ROWS - 8)
        middle = r >= 4 and r + 1 <= ROWS - 4 and rs == r - 4
        n = (9 if middle else 8) * GRID_W
        off = FULL_BIAS if middle else (rs - r + 7 - 1) * GRID_W
        for hh in range(2):
            out.append((hh, t, CTX + rs * GRID_W, n, off))
    for t in range(CT):
        for hh in range(2):
            out.append((hh, t, 0, 0, 0))
    return out


def units_odd(j):
    out = []
    for t in range(2, NT):
        lo, hi = max(t - 1, 2), min(t + 2, NT)
        for hh in range(2):
            out.append((hh, t, lo * P, (hi - lo) * P, (lo - (t - 1)) * P))
    return out


def scan_order(d):
    if d == 0:
        return list(range(NT))
    return list(range(CT - 1, -1, -1)) + list(range(NT - 1, CT - 1, -1))


class Slot:
    pass


def interleave(main, filler):
    out, done, other = [], 0, 0

    def under_way():
        return 0 < done < len(filler) and filler[done][0] == "mm" and filler[done][7] > 0

    for i, s in enumerate(main):
        if s[0] == "lin_turn" and under_way():
            while other and under_way():
                out.append(filler[done])
                done += 1
            other += under_way()
        out.append(s)
        while done < (i + 1) * len(filler) // len(main):
            out.append(filler[done])
            done += 1
            other = other if under_way() else 0
    return out


def project(kind, dest, chunks):
    out = []
    for t0, n in chunks:
        bank, stage = Slot(), Slot()
        out += [("mm", kind, dest, t0, n, bank, stage, part) for part in range(4)]
        if dest in ("v0", "v1", "v", "vv"):
            out.append(("vturn", kind, dest, t0, n, Slot(), stage))
        if dest in ("rq", "kk") and t0 >= CTX:
            out.append(("rope", kind, dest, t0, n, Slot(), stage))
    return out


def attention(l, j, units):
    main, n = [], len(units)

    def scores(i):
        return [(kind, ("att", l, j, i), units[i]) for kind in ("scores", "softmax")] if i < n else []

    main += scores(0) + scores(1)
    for i in range(n + 2):
        if i < n:
            main.append(("ptrans", ("att", l, j, i), units[i]))
        main += scores(i + 2)
        if 0 <= i - 1 < n:
            main.append(("pv", ("att", l, j, i - 1), units[i - 1]))
        if 0 <= i - 2 < n and units[i - 2][0] == 1:
            main.append(("yout", ("att", l, j, i - 2), units[i - 2]))
    return main


def scan(l, p):
    steps = [dict(l=l, p=p, i=i, t=(scan_order(0)[i], scan_order(1)[i]), wanted=(l == 0 or i >= CT))
             for i in range(NT)]
    for q in steps:
        q["second"] = q["t"][0] in scan_order(1)[:q["i"]]
        assert q["second"] == (q["t"][1] in scan_order(0)[:q["i"]])
    main = []
    for x in range(NT + 4):
        now, one, two, three, four = (steps[x - y] if 0 <= x - y < NT else None for y in range(5))
        turned = four and four["second"] and four["wanted"]
        if three:
            main += [("lin_inside", three), ("lin_chunk", three, 0)]
        if two:
            main.append(("lin_attend", two))
        if turned:
            main.append(("lin_norm", four))
        if now and l == 0:
            main.append(("lin_gate", now))
        if one:
            main.append(("lin_scale", one))
        if turned:
            main.append(("lin_turn", four, Slot()))
        if three:
            main += [("lin_chunk", three, 1), ("lin_out", three)]
        if now and l == 0:
            main.append(("lin_log", now))
        if one:
            main.append(("lin_mul", one))
    return main


def ada(l, tiles):
    return [("ada", l, f, Slot()) for f in tiles]


def qkv(group, j, chunks_q=CHUNKS_ALL):
    out = []
    for w in (("q", "k", "v") if group == "na" else ("q", "k", "v0", "v1")):
        out += project((group, j, w), w, chunks_q if w == "q" else CHUNKS_ALL)
    return out


def between(products, extra):
    ends = [i + 1 for i, s in enumerate(products)
            if s[0] != "mm" and (i + 1 == len(products) or products[i + 1][0] == "mm")
            or s[0] == "mm" and s[7] == 3 and (i + 1 == len(products) or products[i + 1][0] == "mm")]
    out, at, used = [], 0, 0
    for n, e in enumerate(ends):
        out += products[at:e]
        at = e
        while used < (n + 1) * len(extra) // len(ends):
            out.append(extra[used])
            used += 1
    return out


def make_schedule():
    s = [("setup",)]
    for k in range(KT):
        s += ada(0, (k, 8 + k)) + [("modulate", k)]
    s += project(("lr",), "lr", CHUNKS_ALL) + qkv("gla", 0)
    s += interleave(scan(0, 0), qkv("gla", 1))
    s += interleave(scan(0, 1), between(qkv("na", 0), ada(0, range(16, 24))))
    for j in range(4):
        if j < 3:
            fill = between(qkv("na", j + 1), ada(1, range(8 * j, 8 * j + 8)))
        else:
            fill = project(("gate", 0, 0), "gate", CHUNKS_ALL) + project(("gate", 0, 1), "gate", CHUNKS_ALL)
        s += interleave(attention(0, j, units_even(j)), fill)
    for f in range(2, 8):
        s += project(("gate", 0, f), "gate", CHUNKS_ALL)
    for f in range(8):
        s += project(("out", 0, f), "out", CHUNKS_ALL)
    s += [("norm", 0, c) for c in range(3)]
    s += project(("gates",), "gates", CHUNKS_ALL)
    s += [("rows",)]
    s += qkv("ml", 0, CHUNKS_LAT)
    s += [("rows_exp",)]
    s += [("rows_turn", t, Slot()) for t in range(NT)]
    s += interleave(scan(1, 0), qkv("ml", 1, CHUNKS_LAT))
    fill = project(("sw", 0, "k"), "kk", CHUNKS_ALL) + project(("sw", 0, "v"), "vv", CHUNKS_ALL)
    s += interleave(scan(1, 1), fill + project(("sw", 0, "q"), "rq", CHUNKS_LAT))
    for j in range(4):
        fill = project(("sw", j + 1, "q"), "rq", CHUNKS_LAT) if j < 3 else []
        s += interleave(attention(1, j, units_odd(j)), fill + project(("gate", 1, j), "gate", CHUNKS_LAT))
    for f in range(4, 8):
        s += project(("gate", 1, f), "gate", CHUNKS_LAT)
    for f in range(8):
        s += project(("out", 1, f), "out", CHUNKS_LAT)
    s += [("norm", 1, c) for c in range(1, 3)]
    banks, stages, out = {}, {}, []
    for st in s:
        st = list(st)
        at = {"mm": 5, "vturn": 5, "rope": 5, "ada": 3, "lin_turn": 2, "rows_turn": 2}.get(st[0])
        if at is not None:
            st[at] = banks.setdefault(st[at], len(banks))
        if st[0] in ("mm", "vturn", "rope"):
            staged = st[2] in ("v0", "v1", "v", "vv", "gate") or (st[2] in ("rq", "kk") and st[3] >= CTX)
            st[6] = stages.setdefault(st[6], len(stages)) if staged else None
        out.append(tuple(st))
    return out


SCHEDULE = make_schedule()
PLAN = []
for _s in SCHEDULE:
    _k = ("ada", _s[1], _s[2]) if _s[0] == "ada" else _s[1] if _s[0] == "mm" else None
    if _k is not None and _k not in PLAN:
        PLAN.append(_k)
WEIGHT_AT = {k: n for n, k in enumerate(PLAN)}
RESID = [s for s in SCHEDULE if s[0] == "mm" and s[2] == "out" and s[7] == 0]
RESID_AT = {(s[1][1], s[1][2], s[3]): i for i, s in enumerate(RESID)}
STAGED = {s[6]: s for s in SCHEDULE if s[0] == "mm" and s[7] == 0 and s[6] is not None}
N_UNITS = (20, 16)


def pair_slot(kind):
    order = [("gla", 0), ("gla", 1), ("na", 0), ("na", 1), ("na", 2), ("na", 3), ("ml", 0), ("ml", 1),
             ("sw", 0), ("sw", 1), ("sw", 2), ("sw", 3)]
    n = order.index(kind[:2])
    return n % 2, (order[n - 2] if n >= 2 else None)


def readers(pair):
    if pair[0] in ("gla", "ml"):
        return [("lin_pe", pair[0] == "ml", pair[1]), ("lin_dve", pair[0] == "ml", pair[1])]
    return [("att_pe", int(pair[0] == "sw"), pair[1])]


def key_chunks(unit):
    hh, t, k0, nk, _o = unit
    full = [(o, P, (k0 + o) // P) for o in range(0, nk - nk % P, P)]
    ctx = [(nk + o, P, o // P) for o in range(0, CTX, P)]
    part = [(nk - nk % P, nk % P, (k0 + nk - nk % P) // P)] if nk % P else []
    return full + ctx + part


def before(uid, n=1):
    _, l, j, i = uid
    i += j * N_UNITS[l] - n
    return None if i < 0 else ("att", l, i // N_UNITS[l], i % N_UNITS[l])


def unit_of(uid):
    return (units_even if uid[1] == 0 else units_odd)(uid[2])[uid[3]]


class Counts:

    def __init__(self, known, sems):
        self.known, self.sems, self.now, self.new = known, sems, {}, {}

    def up(self, name, *keys, by=1):
        self.now[name] = self.now.get(name, 0) + by
        for key in keys:
            assert key not in self.new, key
            self.new[key] = (name, self.now[name])
        return self.sems[name], by

    def at(self, key):
        name, value = self.known[key] if self.known is not None else ("vector_done", 1)
        return self.sems[name], value

    def last(self, name):
        return self.sems[name], self.now[name]


SEMS = (["pool_done", "tensor_done", "vector_done", "scalar_done", "constants_loaded", "tables_loaded", "spill_done",
         "out_done", "residual_loaded0", "residual_loaded1", "bias_loaded0", "bias_loaded1"]
        + [f"x_loaded{k}" for k in range(KT)] + [f"weight_loaded{i}" for i in range(WBUFS)])


def build(nc, a, known):
    with ExitStack() as stack:
        def sb(name, shape):
            return stack.enter_context(nc.sbuf_tensor(name, shape, F32))

        def bank(name, n=1):
            return stack.enter_context(nc.psum_tensor(name, [P, n * 512], F32))

        sems = {n: stack.enter_context(nc.semaphore(n)) for n in SEMS}
        c = Counts(known, sems)
        at, up = c.at, c.up

        hT = sb("hT", [P, KT, T])
        yT = sb("yT", [P, KT, T])
        weights = sb("weights", [P, WBUFS, KT, P])
        pair = sb("pair", [P, 2, 2 * T + NT * 2 * VW])
        kvT = sb("kvT", [P, T])
        kvV = sb("kvV", [P, NT, P])
        consts = sb("consts", [P, CONST_W])
        tables = sb("tables", [P, TABLES_W])
        cols = sb("cols", [P, COLS_W])
        mods = sb("mods", [P, 2, 24, 2])
        vstage = sb("vstage", [P, 2, 512])
        work = sb("work", [P, 4100])
        gate_w = sb("gate_w", [P, 512])
        tokc = sb("tokc", [P, NT, 3, 8])
        rows2 = sb("rows2", [GATE_ROWS, 2, T])
        rowm = sb("rowm", [GATE_ROWS, T // CHUNK])
        stat = sb("stat", [P, 4, 8])
        rstat = sb("rstat", [P, 16])

        PJ = [bank("proj0"), bank("proj1")]
        SC = bank("scores", 2)
        TP = [bank("turned0"), bank("turned1")]
        OV = bank("values")
        MI = bank("misc")

        def const(name):
            o, n = CONST[name]
            return consts[:, o:o + n]

        def col(name, i, n=1):
            o = COLS[name][0] + i
            return cols[:, o:o + n]

        ident = const("ident")

        def pq(slot):
            return pair[:, slot, 0:T]

        def pk(slot):
            return pair[:, slot, T:2 * T]

        def pv(slot):
            return pair[:, slot, 2 * T:].rearrange("p (t h w) -> p t h w", t=NT, h=2)

        def lin_slot(l, p):
            return pair_slot(("ml" if l else "gla", p))[0]

        def att_slot(l, j):
            return pair_slot(("sw" if l else "na", j))[0]

        prob = [work[:, 0:832], work[:, 832:1664]]
        prob_t = [work[:, 1664:1664 + 896], work[:, 2560:2560 + 896]]
        ytok = work[:, 3456:3584]
        LIN = ({"g": 0, "na": 2, "eb0": 4, "eb1": 6, "enb": 8, "ekd": 10, "kin": 12, "kd": 14, "qin": 18, "at": 22},
               {"eb0": 0, "eb1": 2, "w": 4, "qz": 8, "kd": 14, "qin": 18, "at": 22})

        def lin(l, name, n=2):
            o = LIN[l][name] * P
            return work[:, o:o + n * P]

        def buf(q, name):
            o = {"kd": (4, 0), "qin": (4, 512), "at": (5, 0), "qz": (5, 512)}[name]
            return yT[:, o[0], o[1]:o[1] + 512] if q["i"] % 2 else lin(q["l"], name, 4)

        def decays(q):
            n = (q["p"] * NT + q["i"]) % 3
            return yT[:, 4, 1024:1280] if n == 2 else lin(q["l"], f"eb{n}")

        squares = yT[:, 5, 1024:1152]

        def tiles(ap):
            return ap.rearrange("p (x n) -> p x n", n=P)

        state = [work[:, 26 * P + d * VW:26 * P + (d + 1) * VW] for d in range(2)]
        osum = work[:, 26 * P + 2 * VW:26 * P + 2 * VW + 512]
        x_stage = [work[:, 0:512], work[:, 512:1024]]
        sq_stage = [work[:, 1024:1536], work[:, 1536:2048]]
        mean_neg, rstd = work[:, 2048:2560], work[:, 2560:3072]

        def two(ap):
            return ap.rearrange("p (h n) -> p h n", h=2)

        def by_dir(ap):
            return ap.rearrange("p (d h n) -> p d h n", d=2, h=2)

        def over_heads(ap):
            return two(ap).unsqueeze(2).broadcast_to([P, 2, 2, P])

        def y_block(p, t):
            return yT[:, 2 * p:2 * p + 2, t * P:(t + 1) * P]

        def chunk_no(t0):
            return [x[0] for x in CHUNKS_ALL].index(t0)

        def sum_bank(t0):
            return [SC[:, 0:512], SC[:, 512:1024], TP[0][:, :]][chunk_no(t0)]

        def square_bank(ci):
            return [MI, OV, TP[1]][ci]

        def step_before(q, first=0, by=1):
            n = q["p"] * (NT - first) + q["i"] - first - by
            return None if n < 0 else (q["l"], n // (NT - first), n % (NT - first) + first)

        def first_wanted(l):
            return CT if l else 0

        def out_bank(l, d):
            if l:
                return (OV[:, 0:2 * VW], SC[:, 512:512 + 2 * VW])[d]
            return OV[:, d * 2 * P:(d + 1) * 2 * P]

        block = stack.enter_context(nc.Block())

        @block.sync
        def _(sp):
            for name, dst in (("consts", consts), ("cols", cols), ("gate_w", gate_w)):
                sp.dma_start(dst[:, :], a[name]).then_inc(*up("constants_loaded", ("loaded", name), by=16))
            sent = [0, 0]

            def load_weights(upto):
                while sent[0] < min(upto, len(PLAN)):
                    n = sent[0]
                    if n >= WBUFS:
                        sp.wait_ge(*at(("weight_used", n - WBUFS)))
                    sp.dma_start(weights[:, n % WBUFS, :, :], a["weights"][n]).then_inc(
                        *up(f"weight_loaded{n % WBUFS}", ("weight", n), by=16))
                    sent[0] += 1

            def load_bias(j, hh):
                if j >= 1:
                    sp.wait_ge(*at(("softmax_dve", ("att", 0, j - 1, 14 + hh))))
                sp.dma_start(tables[:, hh * BIAS:(hh + 1) * BIAS], a["bias"][2 * j + hh]).then_inc(
                    *up(f"bias_loaded{hh}", ("bias", j, hh), by=16))

            load_weights(2)
            for k in range(KT):
                sp.dma_start(hT[:, k, :], a["xT"][k]).then_inc(*up(f"x_loaded{k}", ("x", k), by=16))
            for s in SCHEDULE:
                if s[0] == "ada":
                    load_weights(WEIGHT_AT[("ada", s[1], s[2])] + WBUFS)
                if s[0] == "mm" and s[7] == 0:
                    if s[2] == "out":
                        l, f, t0, n, i = s[1][1], s[1][2], s[3], s[4], sent[1]
                        if i >= 2:
                            sp.wait_ge(*at(("resid_used", i - 2)))
                        if f == 0 and t0 == (CTX if l else 0):
                            sp.wait_ge(*at(("att_pe", l, 3)))
                            sp.wait_ge(*at(("y_turned_pe", l, 3)))
                            if l:
                                sp.wait_ge(*at(("spill", 2)))
                        src = a["x1T"] if l else a["xT"]
                        sp.dma_start(x_stage[i % 2][:, 0:n], src[f, :, t0:t0 + n]).then_inc(
                            *up(f"residual_loaded{i % 2}", ("resid", i), by=16))
                        sent[1] += 1
                    load_weights(WEIGHT_AT[s[1]] + WBUFS)
                if s[0] == "lin_scale" and s[1]["l"] == 0 and s[1]["p"] == 1 and s[1]["i"] < 2:
                    load_bias(0, s[1]["i"])
                if s[0] == "scores" and s[1][1] == 0 and s[1][2] < 3 and s[1][3] in (16, 17):
                    load_bias(s[1][2] + 1, s[1][3] - 16)
                if s[0] == "norm":
                    l, ci = s[1], s[2]
                    t0, n = CHUNKS_ALL[ci]
                    if l == 0 and ci == 0:
                        sp.wait_ge(*at(("softmax_dve", ("att", 0, 3, 15))))
                        sp.dma_start(tables[:, :], a["tables"]).then_inc(*up("tables_loaded", ("tables",), by=16))
                    sp.wait_ge(*at(("normed", l, ci)))
                    dst, lo = (a["out"], t0 - CTX) if l else (a["x1T"], t0)
                    sp.dma_start(dst[:, :, lo:lo + n].rearrange("k p n -> p k n"), yT[:, :, t0:t0 + n]).then_inc(
                        *(up("out_done", ("stored", ci), by=16) if l else up("spill_done", ("spill", ci), by=16)))
            sp.wait_ge(*at(("spill", 2)))
            sp.wait_ge(*at(("stored", 2)))

        @block.tensor
        def _(pe):
            def done(ins, *keys):
                ins.then_inc(*up("tensor_done", *keys))

            def s_setup():
                pe.wait_ge(*at(("cond",)))

            def s_ada(l, f, u):
                n = WEIGHT_AT[("ada", l, f)]
                pe.wait_ge(*at(("weight", n)))
                if u >= 2:
                    pe.wait_ge(*at(("proj_free", u - 2)))
                for k in range(KT):
                    last = nc.tensor.matmul(PJ[u % 2][:, 0:2], weights[:, n % WBUFS, k, :], col("cond", 2 * k, 2),
                                            start=(k == 0), stop=(k == KT - 1))
                done(last, ("proj", u), ("weight_used", n))

            def column_sum(l, f, t0, n):
                pe.wait_ge(*at(("resid_sum", l, f, t0)))
                last = nc.tensor.matmul(sum_bank(t0)[:, 0:n], const("ones"), hT[:, f, t0:t0 + n],
                                        start=(f == 0), stop=(f == KT - 1), skip_group_check=True)
                if f == KT - 1:
                    done(last, ("sum", l, t0))

            def s_mm(kind, dest, t0, n, u, stage, part):
                w = WEIGHT_AT[kind]
                src = yT if dest == "out" else hT
                if part == 0:
                    pe.wait_ge(*at(("weight", w)))
                    pe.wait_ge(*at(("proj_free", u - 2)))
                    if dest == "gates":
                        pe.wait_ge(*at(("h1", chunk_no(t0))))
                    if dest == "out" and kind[2] == 0:
                        for f in range(KT):
                            pe.wait_ge(*at(("gated", kind[1], f, t0)))
                for k in range(2 * part, 2 * part + 2):
                    if dest == "lr" and t0 == 0:
                        pe.wait_ge(*at(("modulated", k)))
                    last = nc.tensor.matmul(PJ[u % 2][:, 0:n], weights[:, w % WBUFS, k, :], src[:, k, t0:t0 + n],
                                            start=(k == 0), stop=(k == KT - 1))
                if part == 3:
                    done(last, ("proj", u), *([("weight_used", w)] if t0 + n == T else []))
                    if dest == "out":
                        f, l = kind[2], kind[1]
                        if f >= 1:
                            column_sum(l, f - 1, t0, n)
                        if f == KT - 1 and t0 + n == T:
                            for t1, n1 in (CHUNKS_LAT if l else CHUNKS_ALL):
                                column_sum(l, KT - 1, t1, n1)

            def s_norm(l, ci):
                t0, n = CHUNKS_ALL[ci]
                for f in range(KT):
                    pe.wait_ge(*at(("square", l, ci, f)))
                    last = nc.tensor.matmul(square_bank(ci)[:, 0:n], const("ones"), sq_stage[f % 2][:, 0:n],
                                            start=(f == 0), stop=(f == KT - 1))
                    done(last, ("square_used", l, ci, f))

            def s_vturn(kind, dest, t0, n, u, stage):
                pe.wait_ge(*at(("staged", stage)))
                pe.wait_ge(*at(("proj_free", u - 2)))
                for i in range(n // P):
                    last = nc.tensor.transpose(PJ[u % 2][:, i * P:(i + 1) * P],
                                               vstage[:, stage % 2, i * P:(i + 1) * P], ident)
                done(last, ("proj", u), ("stage_used", stage))

            def s_rope(kind, dest, t0, n, u, stage):
                pe.wait_ge(*at(("staged", stage)))
                pe.wait_ge(*at(("proj_free", u - 2)))
                done(nc.tensor.matmul(PJ[u % 2][:, 0:n], const("perm"), vstage[:, stage % 2, 0:n], start=True,
                                      stop=True), ("proj", u))

            def s_scores(uid, unit):
                _, l, j, i = uid
                hh, t, k0, nk, _o = unit
                if i == 0:
                    for w in (("rq",) if l else ("q", "k", "v")):
                        pe.wait_ge(*at(("filled", "sw" if l else "na", j, w)))
                    if l:
                        pe.wait_ge(*at(("filled", "sw", 0, "kk")))
                        pe.wait_ge(*at(("filled", "sw", 0, "vv")))
                    if j == 0:
                        pe.wait_ge(*at(("lin_dve", l, 1)))
                        pe.wait_ge(*at(("lin_act", l, 1)))
                if before(uid):
                    pe.wait_ge(*at(("softmax_dve", before(uid))))
                lo, hi = hh * DH, hh * DH + DH
                q = pq(att_slot(l, j))[lo:hi, t * P:(t + 1) * P]
                keys = kvT[:, :] if l else pk(att_slot(l, j))
                for o in range(0, nk, 512):
                    w = min(512, nk - o)
                    nc.tensor.matmul(SC[:, o:o + w], q, keys[lo:hi, k0 + o:k0 + o + w], start=True, stop=True)
                co = max(512, nk)
                done(nc.tensor.matmul(SC[:, co:co + CTX], q, keys[lo:hi, 0:CTX], start=True, stop=True,
                                      skip_group_check=True), ("scores", uid))

            def s_ptrans(uid, unit):
                pe.wait_ge(*at(("softmax_act", uid)))
                if before(uid):
                    pe.wait_ge(*at(("pt", before(uid), 0)))
                    if len(key_chunks(unit_of(before(uid)))) > 4:
                        pe.wait_ge(*at(("pt", before(uid), 1)))
                    elif before(uid, 2) and len(key_chunks(unit_of(before(uid, 2)))) > 4:
                        pe.wait_ge(*at(("pt", before(uid, 2), 1)))
                chunks = key_chunks(unit)
                for x, (o, w, _t) in enumerate(chunks):
                    last = nc.tensor.transpose(TP[x // 4][0:w, (x % 4) * P:(x % 4 + 1) * P],
                                               prob[uid[3] % 2][:, o:o + w], ident)
                    if x % 4 == 3 or x == len(chunks) - 1:
                        done(last, ("turned", uid, x // 4), *([("turned", uid)] if x == len(chunks) - 1 else []))

            def s_pv(uid, unit):
                _, l, j, i = uid
                hh = unit[0]
                vals = kvV[:, :, :] if l else pv(att_slot(l, j))[:, :, 0, 0:P]
                chunks = key_chunks(unit)
                if before(uid):
                    pe.wait_ge(*at(("att_out", before(uid))))
                for x, (o, w, t) in enumerate(chunks):
                    if x % 4 == 0:
                        pe.wait_ge(*at(("pt", uid, x // 4)))
                    last = nc.tensor.matmul(OV[:, 0:DH], prob_t[i % 2][0:w, x * P:(x + 1) * P],
                                            vals[0:w, t, hh * DH:(hh + 1) * DH], start=(x == 0),
                                            stop=(x == len(chunks) - 1))
                done(last, ("pv", uid), *([("att_pe", l, j)] if i == N_UNITS[l] - 1 else []))

            def s_yout(uid, unit):
                _, l, j, i = uid
                pe.wait_ge(*at(("att_out", uid)))
                if before(uid, 2):
                    pe.wait_ge(*at(("y_copied", before(uid, 2))))
                done(nc.tensor.transpose(MI[:, 0:P], ytok, ident), ("ytok_used", uid),
                     *([("y_turned_pe", l, j)] if i == N_UNITS[l] - 1 else []))

            def s_lin_gate(q):
                p, i = q["p"], q["i"]
                if i == 0:
                    pe.wait_ge(*at(("filled_lr",)))
                    pe.wait_ge(*at(("loaded", "gate_w")))
                if step_before(q):
                    pe.wait_ge(*at(("g", *step_before(q))))
                for d in range(2):
                    r, o, t = slice(32 * d, 32 * d + 17), d * 256 + p * P, q["t"][d]
                    if d:
                        pe.wait_ge(*c.last("tensor_done"))
                    done(nc.tensor.matmul(SC[:, d * P:(d + 1) * P], kvT[r, t * P:(t + 1) * P], gate_w[r, o:o + P],
                                          start=True, stop=True), ("gate", p, i, d))

            def s_lin_scale(q):
                l, p, i = q["l"], q["p"], q["i"]
                if i == 0:
                    for w in ("q", "k", "v0", "v1"):
                        pe.wait_ge(*at(("filled", "ml" if l else "gla", p, w)))
                    if l:
                        pe.wait_ge(*at(("rows_turned", NT - 1)))
                        pe.wait_ge(*at(("tables",)))
                if step_before(q):
                    pe.wait_ge(*at(("scale_act", *step_before(q))))
                    pe.wait_ge(*at(("scale_done", *step_before(q))))
                if l == 0:
                    pe.wait_ge(*at(("g", l, p, i)))
                for d in range(2):
                    cs = slice(q["t"][d] * P, (q["t"][d] + 1) * P)
                    if l == 0:
                        g = lin(0, "g")[:, d * P:(d + 1) * P]
                        nc.tensor.matmul(SC[:, 512 + d * P:640 + d * P], g, const("tri_" + "fb"[d]), start=True,
                                         stop=True)
                        nc.tensor.matmul(SC[:, 768 + d * P:896 + d * P], const("stri_" + "fb"[d]), g, start=True,
                                         stop=True)
                    elif q["wanted"]:
                        for h in range(2):
                            o = SEL_AT + (4 + d * 4 + 2 * p + h) * P
                            last = nc.tensor.matmul(SC[:, (2 * d + h) * P:(2 * d + h + 1) * P],
                                                    tables[0:GATE_ROWS, o:o + P], rows2[:, 0, cs], start=True,
                                                    stop=True)
                        if d:
                            done(last, ("spread", p, i))
                for d in range(2):
                    cs = slice(q["t"][d] * P, (q["t"][d] + 1) * P)
                    if l:
                        o = SEL_AT + (2 * d + p) * P
                        nc.tensor.matmul(MI[:, 256 + d * P:384 + d * P], tables[0:GATE_ROWS, o:o + P],
                                         rows2[:, 1, cs], start=True, stop=True)
                    last = nc.tensor.transpose(MI[:, d * P:(d + 1) * P], pk(lin_slot(l, p))[:, cs], ident)
                done(last, ("scale", l, p, i))

            def s_lin_attend(q):
                if not q["wanted"]:
                    return
                l, p, i = q["l"], q["p"], q["i"]
                pe.wait_ge(*at(("scale_done", l, p, i)))
                if step_before(q, first_wanted(l)):
                    pe.wait_ge(*at(("attend_done", *step_before(q, first_wanted(l)))))
                if l:
                    pe.wait_ge(*at(("q_padded", p, i)))
                for d in range(2):
                    t = q["t"][d]
                    keys = pk(lin_slot(l, p))[:, t * P:(t + 1) * P] if l else lin(0, "kin")[:, d * P:(d + 1) * P]
                    last = nc.tensor.matmul(TP[0][:, 2 * d * P:2 * (d + 1) * P], keys,
                                            buf(q, "qz" if l else "qin")[:, 2 * d * P:2 * (d + 1) * P],
                                            start=True, stop=True)
                done(last, ("attend", l, p, i))

            def s_lin_inside(q):
                if not q["wanted"]:
                    return
                l, p, i = q["l"], q["p"], q["i"]
                vw = VW if l else P
                pe.wait_ge(*at(("attend_done", l, p, i)))
                if step_before(q, first_wanted(l)):
                    pe.wait_ge(*at(("lin_read", *step_before(q, first_wanted(l)))))
                for d in range(2):
                    for h in range(2):
                        o = (2 * d + h) * P
                        last = nc.tensor.matmul(out_bank(l, d)[:, h * vw:(h + 1) * vw], buf(q, "at")[:, o:o + P],
                                                pv(lin_slot(l, p))[:, q["t"][d], h, 0:vw],
                                                start=(h == 0 and (l == 1 or d == 0)), stop=False,
                                                skip_group_check=True)
                done(last, ("inside", l, p, i))

            def s_lin_chunk(q, n):
                l, p, i = q["l"], q["p"], q["i"]
                slot, vw = lin_slot(l, p), (VW if l else P)
                if n == 0:
                    pe.wait_ge(*at(("scale_done", l, p, i)))
                for d in range(2):
                    if n == 0 and i == 0:
                        pe.wait_ge(*at(("state0", l, p)))
                    else:
                        pe.wait_ge(*at(("state", l, p, *((i, 0) if n else (i - 1, 1)), d)))
                    half = n if d == 0 else 1 - n
                    r = slice(half * CHUNK, (half + 1) * CHUNK)
                    for h in range(2) if q["wanted"] else ():
                        queries = buf(q, "qin")[:, (2 * d + h) * P:(2 * d + h + 1) * P][:, r]
                        last = nc.tensor.matmul(out_bank(l, d)[r, h * vw:(h + 1) * vw], queries, state[d][:, 0:vw],
                                                start=False, stop=(n == 1), skip_group_check=True)
                    if q["wanted"]:
                        done(last, ("lin_o", l, p, i, n, d))
                if i == NT - 1 and n == 1:
                    c.new[("lin_pe", bool(l), p)] = c.new[("lin_o", l, p, i, n, 1)]
                    return
                if i == 0 and n == 0 and p:
                    pe.wait_ge(*at(("state", l, 0, NT - 1, 0, 1)))
                for d in range(2):
                    half = n if d == 0 else 1 - n
                    for h in range(2):
                        o = (2 * half + d) * P + h * DH
                        last = nc.tensor.matmul(TP[1][h * DH:(h + 1) * DH, d * vw:(d + 1) * vw],
                                                buf(q, "kd")[:, o:o + DH], pv(slot)[:, q["t"][d], h, 0:vw],
                                                start=True, stop=True, skip_group_check=True)
                done(last, ("update", l, p, i, n))

            def s_lin_turn(q, u):
                l, p, i = q["l"], q["p"], q["i"]
                pe.wait_ge(*at(("lin_y", l, p, i)))
                pe.wait_ge(*at(("proj_free", u - 2)))
                first = 0 if q["t"][0] < q["t"][1] else 1
                for h in range(2):
                    for x in range(2):
                        d = first if x == 0 else 1 - first
                        last = nc.tensor.transpose(PJ[u % 2][:, (2 * h + x) * P:(2 * h + x + 1) * P],
                                                   osum[:, (2 * d + h) * P:(2 * d + h + 1) * P], ident)
                done(last, ("proj", u), ("osum_used", l, p, i))

            def s_rows_turn(t, u):
                if t == 0:
                    pe.wait_ge(*at(("rows_act",)))
                    pe.wait_ge(*at(("rows_dve",)))
                pe.wait_ge(*at(("proj_free", u - 2)))
                for i, k in enumerate((0, 6, 7)):
                    last = nc.tensor.transpose(PJ[u % 2][:, i * GATE_ROWS:(i + 1) * GATE_ROWS],
                                               yT[0:GATE_ROWS, k, t * P:(t + 1) * P],
                                               ident[0:GATE_ROWS, 0:GATE_ROWS])
                done(last, ("proj", u))

            part = {"setup": s_setup, "ada": s_ada, "mm": s_mm, "vturn": s_vturn, "rope": s_rope, "scores": s_scores,
                    "ptrans": s_ptrans, "pv": s_pv, "yout": s_yout, "lin_gate": s_lin_gate,
                    "lin_scale": s_lin_scale, "lin_attend": s_lin_attend,
                    "lin_inside": s_lin_inside, "lin_chunk": s_lin_chunk, "lin_turn": s_lin_turn, "rows_turn": s_rows_turn, "norm": s_norm}
            for s in SCHEDULE:
                if s[0] in part:
                    part[s[0]](*s[1:])

        @block.vector
        def _(dve):
            V = nc.vector

            def link(ins, *keys):
                ins.then_inc(*up("vector_done", *keys))
                dve.wait_ge(*c.last("vector_done"))

            def s_setup():
                link(V.memset(kvT[:, :], 1.0), ("lr_ones",))
                for slot in range(2):
                    link(V.memset(pv(slot)[:, :, :, P:VW], 1.0), ("v_ones", slot))
                dve.wait_ge(*at(("cond_exp",)))
                cond = col("cond", 0, 16)
                link(V.tensor_scalar(rstat[:, :], rstat[:, :], 1.0, None, ALU.add))
                link(V.reciprocal(rstat[:, :], rstat[:, :]))
                link(V.tensor_tensor(cond, cond, rstat[:, :], ALU.mult), ("cond",))

            def s_ada(l, f, u):
                dve.wait_ge(*at(("proj", u)))
                link(V.tensor_scalar(mods[:, l, f, :], PJ[u % 2][:, 0:2], col("b_ada", l * 24 + f),
                                     1.0 if 8 <= f < 16 else 0.0, ALU.add, ALU.add), ("proj_free", u), ("mods", l, f))

            def s_modulate(k):
                dve.wait_ge(*at(("x", k)))
                for w, (t0, n) in ((1, (0, CTX)), (0, (CTX, LAT))):
                    link(V.tensor_scalar(hT[:, k, t0:t0 + n], hT[:, k, t0:t0 + n], mods[:, 0, 8 + k, w:w + 1],
                                         mods[:, 0, k, w:w + 1], ALU.mult, ALU.add),
                         *([] if w else [("modulated", k)]))

            def s_mm(kind, dest, t0, n, u, stage, part):
                if part != 3:
                    return
                ps = PJ[u % 2][:, 0:n]
                if dest == "gate":
                    l, f = kind[1], kind[2]
                    e, y = vstage[:, stage % 2, 0:n], yT[:, f, t0:t0 + n]
                    dve.wait_ge(*at(("staged", stage)))
                    link(V.tensor_scalar(e, e, 1.0, None, ALU.add))
                    link(V.reciprocal(e, e))
                    link(V.tensor_tensor(e, ps, e, ALU.mult), ("proj_free", u))
                    dve.wait_ge(*at(("y_turned", l, f)))
                    link(V.tensor_tensor(y, y, e, ALU.mult), ("gated", l, f, t0), ("stage_used", stage))
                elif dest == "out":
                    l, f = kind[1], kind[2]
                    i = RESID_AT[(l, f, t0)]
                    dve.wait_ge(*at(("proj", u)))
                    dve.wait_ge(*at(("resid_scaled", i)))
                    w = 1 if t0 == 0 else 0
                    link(V.scalar_tensor_tensor(out=hT[:, f, t0:t0 + n], in0=ps, scalar=mods[:, l, 16 + f, w:w + 1],
                                                in1=x_stage[i % 2][:, 0:n], op0=ALU.mult, op1=ALU.add),
                         ("proj_free", u), ("resid_sum", l, f, t0), ("resid_used", i))

            def s_vturn(kind, dest, t0, n, u, stage):
                if kind[:2] == ("ml", 0):
                    return
                dve.wait_ge(*at(("proj", u)))
                nt, t = n // P, t0 // P
                ps = PJ[u % 2][:, 0:n].rearrange("p (t n) -> p t n", n=P)
                if dest == "vv":
                    dst = kvV[:, t:t + nt, :]
                    keys = [("filled", "sw", 0, "vv")]
                else:
                    slot, prev = pair_slot(kind)
                    for r in readers(prev) if prev and t0 == 0 else []:
                        dve.wait_ge(*at(r))
                    dst = pv(slot)[:, t:t + nt, 1 if dest == "v1" else 0, 0:P]
                    keys = [("filled", kind[0], kind[1], dest)]
                link(V.tensor_copy(dst, ps), ("proj_free", u), *(keys if t0 + n == T else []))

            def s_rope(kind, dest, t0, n, u, stage):
                dve.wait_ge(*at(("proj", u)))
                if kind == ("sw", 0, "k") and t0 == CTX:
                    dve.wait_ge(*at(("tables",)))
                st = vstage[:, stage % 2, 0:n]
                ps = PJ[u % 2][:, 0:n]
                if dest == "kk":
                    dst, key = kvT[:, t0:t0 + n], ("filled", "sw", 0, "kk")
                else:
                    slot, prev = pair_slot(kind)
                    for r in readers(prev) if t0 == CTX else []:
                        dve.wait_ge(*at(r))
                    dst, key = pq(slot)[:, t0:t0 + n], ("filled", "sw", kind[1], "rq")
                lo = t0 - CTX
                link(V.tensor_tensor(dst, ps, tables[:, LAT + lo:LAT + lo + n], ALU.mult), ("proj_free", u))
                link(V.tensor_tensor(st, st, tables[:, lo:lo + n], ALU.mult))
                link(V.tensor_tensor(dst, dst, st, ALU.add), ("stage_used", stage), *([key] if t0 + n == T else []))

            def s_softmax(uid, unit):
                _, l, j, i = uid
                hh, t, k0, nk, bo = unit
                st = stat[:, i % 4, :]
                dve.wait_ge(*at(("scores", uid)))
                if before(uid, 2):
                    dve.wait_ge(*at(("turned", before(uid, 2))))
                if l == 0 and i < 2:
                    dve.wait_ge(*at(("bias", j, hh)))
                co = max(512, nk)
                link(V.tensor_scalar(prob[i % 2][:, nk:nk + CTX], SC[:, co:co + CTX], 0.0, None, ALU.add, ALU.max,
                                     accum_out=st[:, 1:2]))
                if nk:
                    bias = const("band")[:, bo:bo + nk] if l else tables[:, hh * BIAS + bo:hh * BIAS + bo + nk]
                    link(V.tensor_tensor_reduce(prob[i % 2][:, 0:nk], SC[:, 0:nk], bias, 1.0, LOWEST, ALU.add,
                                                ALU.max, st[:, 0:1]))
                if l:
                    link(V.tensor_scalar(st[:, 0:1], st[:, 0:1], col("sink", j + 4 * hh), None, ALU.max))
                link(V.tensor_scalar(st[:, 2:3], st[:, 1:2], st[:, 0:1] if nk else LOWEST, -1.0, ALU.max, ALU.mult),
                     ("softmax_dve", uid))

            def s_ptrans(uid, unit):
                chunks = key_chunks(unit)
                if len(chunks) <= 4:
                    return
                dve.wait_ge(*at(("turned", uid, 1)))
                if before(uid, 2):
                    dve.wait_ge(*at(("pv", before(uid, 2))))
                pt = prob_t[uid[3] % 2]
                whole = [x for x in chunks[4:] if x[1] == P]
                n = len(whole) * P
                half = len(whole) < len(chunks) - 4
                link(V.tensor_copy(pt[:, 512:512 + n], TP[1][:, 0:n]), *([] if half else [("pt", uid, 1)]))
                if half:
                    w = chunks[-1][1]
                    link(V.tensor_copy(pt[0:w, 512 + n:512 + n + P], TP[1][0:w, n:n + P]), ("pt", uid, 1))

            def s_pv(uid, unit):
                _, l, j, i = uid
                hh = unit[0]
                st = stat[:, i % 4, :]
                dve.wait_ge(*at(("softmax_act", uid)))
                if l:
                    link(V.tensor_tensor(st[:, 4:5], st[:, 4:5], st[:, 5:6], ALU.add))
                link(V.reciprocal(st[:, 6:7], st[:, 4:5]))
                dve.wait_ge(*at(("pv", uid)))
                if hh == 0 and before(uid):
                    dve.wait_ge(*at(("ytok_used", before(uid))))
                link(V.tensor_scalar(ytok[:, hh * DH:(hh + 1) * DH], OV[:, 0:DH], st[:, 6:7], None, ALU.mult),
                     ("att_out", uid))

            def s_lin_log(q):
                p, i = q["p"], q["i"]
                dve.wait_ge(*at(("gate_log", p, i)))
                if step_before(q):
                    dve.wait_ge(*at(("scale", *step_before(q))))
                link(V.scalar_tensor_tensor(out=lin(0, "g"), in0=SC[:, 0:2 * P], scalar=0.0, in1=lin(0, "na"),
                                            op0=ALU.min, op1=ALU.subtract), ("g", 0, p, i))

            def s_lin_scale(q):
                l, p, i = q["l"], q["p"], q["i"]
                if i == 0:
                    if step_before(q):
                        dve.wait_ge(*at(("lin_pe", bool(l), 0)))
                    for name in (("kd", "qin") + (("qz",) if l else ())) if p == 0 else ():
                        for odd in range(2):
                            link(V.memset(buf(dict(l=l, i=odd), name), 0.0),
                                 *([("q_zero", 0)] if name == "qz" and odd else []))
                    for d in range(2):
                        link(V.memset(state[d], 0.0), *([("state0", l, p)] if d else []))
                if l and q["wanted"]:
                    dve.wait_ge(*at(("spread", p, i)))
                    link(V.tensor_tensor(by_dir(lin(1, "w", 4)), by_dir(SC[:, 0:4 * P]), over_heads(const("add")),
                                         ALU.add), ("masked", p, i))

            def s_lin_mul(q):
                l, p, i = q["l"], q["p"], q["i"]
                slot = lin_slot(l, p)
                dve.wait_ge(*at(("scale_act", l, p, i)))
                if i >= 2:
                    dve.wait_ge(*at(("update", l, p, i - 2, 1)))
                kd = buf(q, "kd").rearrange("p (c d n) -> p c d n", c=2, d=2)
                for half in range(2):
                    r = slice(half * CHUNK, (half + 1) * CHUNK)
                    if l == 0:
                        link(V.tensor_tensor(kd[r, half, :, :], two(MI[r, 0:2 * P]), two(lin(0, "ekd"))[r, :, :],
                                             ALU.mult))
                        continue
                    for d in range(2):
                        ws = tokc[r, q["t"][d], 1, d * 4 + 2 * p:d * 4 + 2 * p + 2].unsqueeze(2)
                        link(V.tensor_tensor(kd[r, half, d, :].rearrange("p (h n) -> p h n", h=2),
                                             MI[r, d * P:(d + 1) * P].rearrange("p (h n) -> p h n", h=2),
                                             ws.broadcast_to([CHUNK, 2, DH]), ALU.mult),
                             *([("scale_done", l, p, i)] if half and d and not q["wanted"] else []))
                if not q["wanted"]:
                    return
                qin = buf(q, "qin")
                for d in range(2):
                    t = q["t"][d]
                    cs, ds = slice(t * P, (t + 1) * P), slice(d * P, (d + 1) * P)
                    if l == 0:
                        link(V.tensor_tensor(lin(0, "kin")[:, ds], pk(slot)[:, cs], lin(0, "enb")[:, ds], ALU.mult))
                    for h in range(2):
                        r, o = slice(h * DH, (h + 1) * DH), (2 * d + h) * P
                        link(V.tensor_tensor(qin[r, o:o + P], pq(slot)[r, cs], decays(q)[r, ds], ALU.mult),
                             *([("scale_done", l, p, i)] if d and h else []))

            def s_lin_attend(q):
                if not q["wanted"]:
                    return
                l, p, i = q["l"], q["p"], q["i"]
                dve.wait_ge(*at(("attend", l, p, i)))
                if step_before(q, first_wanted(l), 2):
                    dve.wait_ge(*at(("inside", *step_before(q, first_wanted(l), 2))))
                other = by_dir(lin(1, "w", 4)) if l else over_heads(const("mask"))
                link(V.tensor_tensor(by_dir(buf(q, "at")), by_dir(TP[0][:, 0:4 * P]), other, ALU.mult),
                     ("attend_done", l, p, i))

            def s_lin_chunk(q, n):
                l, p, i = q["l"], q["p"], q["i"]
                if i == NT - 1 and n == 1:
                    return
                vw = VW if l else P
                dve.wait_ge(*at(("update", l, p, i, n)))
                for d in range(2):
                    half = n if d == 0 else 1 - n
                    o = d * P + half * CHUNK + (CHUNK - 1 if d == 0 else 0)
                    link(V.scalar_tensor_tensor(out=state[d][:, 0:vw], in0=state[d][:, 0:vw],
                                                scalar=decays(q)[:, o:o + 1], in1=TP[1][:, d * vw:(d + 1) * vw],
                                                op0=ALU.mult, op1=ALU.add), ("state", l, p, i, n, d))

            def s_lin_out(q):
                l, p, i = q["l"], q["p"], q["i"]
                if not q["wanted"]:
                    return
                dve.wait_ge(*at(("lin_o", l, p, i, 1, 1)))
                keys = [("lin_read", l, p, i)] + ([("lin_dve", bool(l), p)] if i == NT - 1 else [])
                if q["second"]:
                    prev = max([y for y in range(i) if y in second_steps(l)], default=None)
                    if prev is not None:
                        dve.wait_ge(*at(("osum_used", l, p, prev)))
                    elif p:
                        dve.wait_ge(*at(("osum_used", l, 0, NT - 1)))
                    else:
                        pass
                if l == 0:
                    for d in range(2):
                        o, y = two(out_bank(0, d)), y_block(p, q["t"][d])
                        if q["second"]:
                            link(V.tensor_tensor(two(osum[:, 2 * d * P:2 * (d + 1) * P]), o, y, ALU.add),
                                 *(keys if d else []))
                        else:
                            link(V.tensor_copy(y, o), *(keys if d else []))
                    return
                r = rstat[:, 8:12]
                outs = [out_bank(1, d).rearrange("p (h w) -> p h w", h=2) for d in range(2)]
                for d in range(2):
                    den, em = outs[d][:, :, P], tokc[:, q["t"][d], 2, d * 4 + 2 * p:d * 4 + 2 * p + 2]
                    link(V.scalar_tensor_tensor(out=r[:, 2 * d:2 * d + 2], in0=den, scalar=-1.0, in1=em,
                                                op0=ALU.mult, op1=ALU.max))
                    link(V.tensor_tensor(r[:, 2 * d:2 * d + 2], den, r[:, 2 * d:2 * d + 2], ALU.max))
                link(V.reciprocal(r, r))
                for d in range(2):
                    for h in range(2):
                        kk = keys if d and h else []
                        y, o, ri = y_block(p, q["t"][d])[:, h, :], outs[d][:, h, 0:P], r[:, 2 * d + h:2 * d + h + 1]
                        if q["second"]:
                            link(V.scalar_tensor_tensor(out=osum[:, (2 * d + h) * P:(2 * d + h + 1) * P], in0=o,
                                                        scalar=ri, in1=y, op0=ALU.mult, op1=ALU.add), *kk)
                        else:
                            link(V.tensor_scalar(y, o, ri, None, ALU.mult), *kk)

            def second_steps(l):
                return [1] * (l == 0) + list(range(CT + (NT - CT) // 2, NT))

            def s_lin_norm(q):
                l, p, i = q["l"], q["p"], q["i"]
                dve.wait_ge(*at(("rms", l, p, i)))
                scale = rstat[:, 4:8].unsqueeze(2).broadcast_to([P, 4, P])
                link(V.tensor_tensor(tiles(osum), tiles(osum), scale, ALU.mult), ("lin_y", l, p, i))

            def s_rows():
                dve.wait_ge(*at(("gates_filled",)))
                R = [yT[0:GATE_ROWS, k, :] for k in range(KT)]
                C = [x.rearrange("p (c n) -> p c n", n=CHUNK) for x in R]
                link(V.scalar_tensor_tensor(out=R[2], in0=R[1], scalar=-1.0, in1=R[1], op0=ALU.mult, op1=ALU.min),
                     ("rows_abs",))
                dve.wait_ge(*at(("rows_log",)))
                link(V.scalar_tensor_tensor(out=R[1], in0=R[1], scalar=0.0, in1=R[2], op0=ALU.min, op1=ALU.subtract))

                def running(src, dst, op, by):
                    f, b = slice(0, 32), slice(32, 64)
                    link(V.tensor_tensor(C[dst][f, :, by:], C[src][f, :, by:], C[src][f, :, :CHUNK - by], op))
                    link(V.tensor_copy(C[dst][f, :, :by], C[src][f, :, :by]))
                    link(V.tensor_tensor(C[dst][b, :, :CHUNK - by], C[src][b, :, :CHUNK - by], C[src][b, :, by:], op))
                    link(V.tensor_copy(C[dst][b, :, CHUNK - by:], C[src][b, :, CHUNK - by:]))

                for n in range(6):
                    running(1 + n % 2, 2 - n % 2, ALU.add, 1 << n)
                link(V.tensor_tensor(R[0], R[0], R[1], ALU.subtract))
                for n in range(6):
                    running(0 if n == 0 else 3 - n % 2, 2 + n % 2, ALU.max, 1 << n)
                link(V.memset(rowm[:, :], 0.0))
                for d in range(2):
                    r = slice(32 * d, 32 * d + 32)
                    e = CHUNK - 1 if d == 0 else 0
                    order = [2 * t + (h if d == 0 else 1 - h) for t in scan_order(d) for h in range(2)]
                    for x, y in zip(order, order[1:]):
                        link(V.scalar_tensor_tensor(out=rowm[r, y:y + 1], in0=rowm[r, x:x + 1],
                                                    scalar=C[3][r, x, e:e + 1], in1=C[1][r, x, e:e + 1],
                                                    op0=ALU.max, op1=ALU.add))
                m = rowm[:, :].unsqueeze(2).broadcast_to([GATE_ROWS, T // CHUNK, CHUNK])
                u = rows2[:, 0, :]
                uc = u.rearrange("p (c n) -> p c n", n=CHUNK)
                link(V.tensor_tensor(uc, C[3], m, ALU.max))
                link(V.tensor_scalar(u, u, -1.0, None, ALU.mult))
                link(V.tensor_tensor(rows2[:, 1, :].rearrange("p (c n) -> p c n", n=CHUNK), uc, m, ALU.add))
                for d in range(2):
                    r = slice(32 * d, 32 * d + 32)
                    e = CHUNK - 1 if d == 0 else 0
                    ul = uc[r, :, e:e + 1].broadcast_to([32, T // CHUNK, CHUNK])
                    link(V.tensor_tensor(C[6][r, :, :], C[0][r, :, :], ul, ALU.add))
                link(V.tensor_tensor(R[7], u, R[1], ALU.subtract), ("rows_dve",))

            def s_norm(l, ci):
                t0, n = CHUNKS_ALL[ci]
                dve.wait_ge(*at(("sum", l, t0)))
                if ci > (1 if l else 0):
                    dve.wait_ge(*at(("normed", l, ci - 1)))
                link(V.tensor_scalar(mean_neg[:, 0:n], sum_bank(t0)[:, 0:n], -1.0 / D, None, ALU.mult))
                for f in range(KT):
                    h = hT[:, f, t0:t0 + n]
                    link(V.tensor_tensor(h, h, mean_neg[:, 0:n], ALU.add), ("centred", l, ci, f))
                dve.wait_ge(*at(("rstd", l, ci)))
                for f in range(KT):
                    h = hT[:, f, t0:t0 + n]
                    link(V.tensor_tensor(h, h, rstd[:, 0:n], ALU.mult), ("scaled", l, ci, f))
                if l == 0:
                    w = 1 if t0 == 0 else 0
                    for f in range(KT):
                        dve.wait_ge(*at(("x_after", l, ci, f)))
                        link(V.tensor_scalar(hT[:, f, t0:t0 + n], yT[:, f, t0:t0 + n], mods[:, 1, 8 + f, w:w + 1],
                                             mods[:, 1, f, w:w + 1], ALU.mult, ALU.add),
                             *([("h1", ci)] if f == KT - 1 else []))

            part = {"setup": s_setup, "ada": s_ada, "modulate": s_modulate, "mm": s_mm, "vturn": s_vturn,
                    "rope": s_rope, "softmax": s_softmax, "ptrans": s_ptrans, "pv": s_pv,
                    "lin_log": s_lin_log, "lin_scale": s_lin_scale, "lin_mul": s_lin_mul,
                    "lin_attend": s_lin_attend, "lin_chunk": s_lin_chunk, "lin_out": s_lin_out, "lin_norm": s_lin_norm, "rows": s_rows,
                    "norm": s_norm}
            for s in SCHEDULE:
                if s[0] in part:
                    part[s[0]](*s[1:])

        @block.scalar
        def _(act):
            def link(ins, *keys):
                ins.then_inc(*up("scalar_done", *keys))
                act.wait_ge(*c.last("scalar_done"))

            def run(out, in_, func, keys=(), **kw):
                link(nc.scalar.activation(out, in_, func, **kw), *keys)

            def s_setup():
                nc.scalar.preload_act_table_set("natural_log_exp_and_others")
                act.wait_ge(*at(("loaded", "gate_w")))
                run(rstat[:, :], col("cond", 0, 16), ACT.Exp, [("cond_exp",)], scale=-1.0)

            def s_mm(kind, dest, t0, n, u, stage, part):
                if part != 3:
                    return
                ps = PJ[u % 2][:, 0:n]
                if dest == "out":
                    i = RESID_AT[(kind[1], kind[2], t0)]
                    act.wait_ge(*at(("resid", i)))
                    run(x_stage[i % 2][:, 0:n], x_stage[i % 2][:, 0:n], ACT.Copy, [("resid_scaled", i)], scale=ALPHA)
                    return
                act.wait_ge(*at(("proj", u)))
                if stage is not None:
                    if stage >= 2:
                        act.wait_ge(*at(("stage_used", stage - 2)))
                    st = vstage[:, stage % 2, 0:n]
                    if dest == "gate":
                        run(st, ps, ACT.Exp, [("staged", stage)], scale=-1.0)
                    else:
                        run(st, ps, ACT.Copy, [("staged", stage), ("proj_free", u)],
                            scale=QSCALE if dest == "rq" else 1.0)
                elif dest == "lr":
                    act.wait_ge(*at(("lr_ones",)))
                    run(kvT[0:16, t0:t0 + n], PJ[u % 2][0:16, 0:n], ACT.Copy)
                    run(kvT[32:48, t0:t0 + n], PJ[u % 2][32:48, 0:n], ACT.Copy,
                        [("proj_free", u)] + ([("filled_lr",)] if t0 + n == T else []))
                elif dest == "gates":
                    act.wait_ge(*at(("spill", 2)))
                    for k in range(2):
                        r = slice(k * GATE_ROWS, (k + 1) * GATE_ROWS)
                        run(yT[0:GATE_ROWS, k, t0:t0 + n], PJ[u % 2][r, 0:n], ACT.Identity,
                            ([("proj_free", u)] + ([("gates_filled",)] if t0 + n == T else [])) if k else [],
                            bias=cols[r, COLS["gate_b"][0]:COLS["gate_b"][0] + 1])
                elif dest == "kk":
                    act.wait_ge(*at(("lin_pe", False, 1)))
                    run(kvT[:, t0:t0 + n], ps, ACT.Copy, [("proj_free", u)])
                else:
                    slot, prev = pair_slot(kind)
                    for r in readers(prev) if prev and t0 in (0, CTX) else []:
                        act.wait_ge(*at(r))
                    dst = (pq if dest == "q" else pk)(slot)[:, t0:t0 + n]
                    scaled = dest == ("k" if kind[0] == "ml" else "q")
                    run(dst, ps, ACT.Copy, [("proj_free", u)] + ([("filled", *kind)] if t0 + n == T else []),
                        scale=QSCALE if scaled else 1.0)

            def s_vturn(kind, dest, t0, n, u, stage):
                if kind[:2] != ("ml", 0):
                    return
                slot, prev = pair_slot(kind)
                act.wait_ge(*at(("proj", u)))
                for r in readers(prev) if t0 == 0 else []:
                    act.wait_ge(*at(r))
                nt, t = n // P, t0 // P
                run(pv(slot)[:, t:t + nt, 1 if dest == "v1" else 0, 0:P],
                    PJ[u % 2][:, 0:n].rearrange("p (t n) -> p t n", n=P), ACT.Copy,
                    [("proj_free", u)] + ([("filled", *kind)] if t0 + n == T else []))

            def s_softmax(uid, unit):
                _, l, j, i = uid
                hh, nk = unit[0], unit[3]
                st, pr = stat[:, i % 4, :], prob[i % 2][:, 0:nk + CTX]
                act.wait_ge(*at(("softmax_dve", uid)))
                if l:
                    run(st[:, 5:6], col("sink", j + 4 * hh), ACT.Exp, bias=st[:, 2:3])
                run(pr, pr, ACT.Exp, [("softmax_act", uid)], bias=st[:, 2:3], accum_out=st[:, 4:5])

            def s_ptrans(uid, unit):
                act.wait_ge(*at(("turned", uid, 0)))
                if before(uid, 2):
                    act.wait_ge(*at(("pv", before(uid, 2))))
                n = min(len(key_chunks(unit)), 4) * P
                run(prob_t[uid[3] % 2][:, 0:n], TP[0][:, 0:n], ACT.Copy, [("pt", uid, 0)])

            def s_yout(uid, unit):
                _, l, j, i = uid
                t = unit[1]
                act.wait_ge(*at(("ytok_used", uid)))
                run(yT[:, 4 + j, t * P:(t + 1) * P], MI[:, 0:P], ACT.Copy,
                    [("y_copied", uid)] + ([("y_turned", l, 4 + j)] if i == N_UNITS[l] - 1 else []))

            def s_lin_gate(q):
                p, i, na = q["p"], q["i"], lin(0, "na")
                act.wait_ge(*at(("gate", p, i, 1)))
                if step_before(q):
                    act.wait_ge(*at(("g", *step_before(q))))
                run(na, SC[:, 0:2 * P], ACT.Abs)
                run(na, na, ACT.Exp, scale=-1.0)
                run(na, na, ACT.Ln, [("gate_log", p, i)], bias=col("one", 0))

            def s_lin_scale(q):
                l, p, i = q["l"], q["p"], q["i"]
                act.wait_ge(*at(("scale", l, p, i)))
                if i >= 3:
                    act.wait_ge(*at(("state", l, p, i - 3, 1, 1)))
                elif p:
                    act.wait_ge(*at(("state", l, 0, NT - 1, 0, 1)))
                if l == 0:
                    if step_before(q):
                        act.wait_ge(*at(("scale_done", *step_before(q))))
                    run(lin(0, "ekd"), SC[:, 768:1024], ACT.Exp)
                    run(decays(q), SC[:, 512:768], ACT.Exp)
                    run(lin(0, "enb"), SC[:, 512:768], ACT.Exp, [("scale_act", l, p, i)], scale=-1.0)
                    return
                run(decays(q), MI[:, 256:512], ACT.Copy, [] if q["wanted"] else [("scale_act", l, p, i)])
                if q["wanted"]:
                    act.wait_ge(*at(("masked", p, i)))
                    for d in range(2):
                        for h in range(2):
                            o, hc = (2 * d + h) * P, d * 4 + 2 * p + h
                            w = lin(1, "w", 4)[:, o:o + P]
                            run(w, w, ACT.Exp, [("scale_act", l, p, i)] if d and h else [],
                                bias=tokc[:, q["t"][d], 0, hc:hc + 1])

            def s_lin_out(q):
                if not (q["second"] and q["wanted"]):
                    return
                l, p, i = q["l"], q["p"], q["i"]
                act.wait_ge(*at(("lin_read", l, p, i)))
                for x in range(4):
                    run(squares, osum[:, x * P:(x + 1) * P], ACT.Square, accum_out=rstat[:, x:x + 1])
                run(rstat[:, 0:4], rstat[:, 0:4], ACT.Ln, scale=1.0 / P, bias=col("eps", 1))
                run(rstat[:, 4:8], rstat[:, 0:4], ACT.Exp, [("rms", l, p, i)], scale=-0.5)

            def s_lin_turn(q, u):
                l, p, i = q["l"], q["p"], q["i"]
                act.wait_ge(*at(("proj", u)))
                lo, hi = sorted(q["t"])
                for h in range(2):
                    f = 2 * p + h
                    keys = []
                    if h:
                        keys = [("proj_free", u)]
                        if i == NT - 1:
                            keys += [("y_turned", l, 2 * p), ("y_turned", l, 2 * p + 1), ("lin_act", l, p)]
                    run(yT[:, f, :].rearrange("p (t n) -> p t n", n=P)[:, lo:hi + 1:hi - lo, :],
                        two(PJ[u % 2][:, 2 * h * P:2 * (h + 1) * P]), ACT.Copy, keys, scale=col("norm_g", l * 4 + f))

            def s_rows():
                R = [yT[0:GATE_ROWS, k, :] for k in range(KT)]
                act.wait_ge(*at(("rows_abs",)))
                run(R[2], R[2], ACT.Exp)
                run(R[2], R[2], ACT.Ln, [("rows_log",)], bias=cols[0:GATE_ROWS, COLS["one"][0]:COLS["one"][0] + 1])

            def s_rows_exp():
                R = [yT[0:GATE_ROWS, k, :] for k in range(KT)]
                act.wait_ge(*at(("rows_dve",)))
                run(rows2[:, 1, :], rows2[:, 1, :], ACT.Exp)
                run(R[6], R[6], ACT.Exp)
                run(R[7], R[7], ACT.Exp, [("rows_act",)])

            def s_rows_turn(t, u):
                act.wait_ge(*at(("proj", u)))
                src = PJ[u % 2][:, 0:3 * GATE_ROWS].rearrange("p (i g r) -> p i g r", i=3, g=2)[:, :, :, 0:4]
                for i in range(3):
                    run(tokc[:, t, i, :].rearrange("p (g r) -> p g r", g=2), src[:, i, :, :], ACT.Copy,
                        [("proj_free", u), ("rows_turned", t)] if i == 2 else [])

            def s_norm(l, ci):
                t0, n = CHUNKS_ALL[ci]
                for f in range(KT):
                    act.wait_ge(*at(("centred", l, ci, f)))
                    if f >= 2:
                        act.wait_ge(*at(("square_used", l, ci, f - 2)))
                    run(sq_stage[f % 2][:, 0:n], hT[:, f, t0:t0 + n], ACT.Square, [("square", l, ci, f)])
                act.wait_ge(*at(("square_used", l, ci, KT - 1)))
                run(rstd[:, 0:n], square_bank(ci)[:, 0:n], ACT.Ln, scale=1.0 / D, bias=col("eps", 0))
                run(rstd[:, 0:n], rstd[:, 0:n], ACT.Exp, [("rstd", l, ci)], scale=-0.5)
                for f in range(KT):
                    act.wait_ge(*at(("scaled", l, ci, f)))
                    run(yT[:, f, t0:t0 + n], hT[:, f, t0:t0 + n], ACT.Identity,
                        [("x_after", l, ci, f)] + ([("normed", l, ci)] if f == KT - 1 else []),
                        scale=col("ln_g", l * 8 + f), bias=col("ln_b", l * 8 + f))

            part = {"setup": s_setup, "mm": s_mm, "vturn": s_vturn, "softmax": s_softmax, "ptrans": s_ptrans, "yout": s_yout,
                    "lin_gate": s_lin_gate, "lin_scale": s_lin_scale, "lin_out": s_lin_out, "lin_turn": s_lin_turn,
                    "rows": s_rows, "rows_exp": s_rows_exp, "rows_turn": s_rows_turn, "norm": s_norm}
            for s in SCHEDULE:
                if s[0] in part:
                    part[s[0]](*s[1:])

        @block.gpsimd
        def _(pool):
            def s_lin_mul(q):
                l, p, i = q["l"], q["p"], q["i"]
                if l == 0 or not q["wanted"]:
                    return
                pool.wait_ge(*at(("q_zero", 0)))
                if p:
                    pool.wait_ge(*at(("lin_pe", True, 0)))
                pool.wait_ge(*at(("filled", "ml", p, "q")))
                if i >= CT + 2:
                    pool.wait_ge(*at(("attend", 1, p, i - 2)))
                for d in range(2):
                    t = q["t"][d]
                    for h in range(2):
                        r, o = slice(h * DH, (h + 1) * DH), (2 * d + h) * P
                        pool.tensor_copy(buf(q, "qz")[r, o:o + P],
                                         pq(lin_slot(1, p))[r, t * P:(t + 1) * P]).then_inc(
                            *up("pool_done", *([("q_padded", p, i)] if d and h else [])))

            part = {"lin_mul": s_lin_mul}
            for s in SCHEDULE:
                if s[0] in part:
                    part[s[0]](*s[1:])

    return c.new


def constants():
    i = np.arange(P)
    same = (i[:, None] // CHUNK) == (i[None, :] // CHUNK)
    s, t = i[:, None], i[None, :]
    parts = {
        "ident": np.eye(P), "ones": np.ones((P, P)),
        "tri_f": same * (s <= t) / GLA_TAU, "tri_b": same * (s >= t) / GLA_TAU,
        "stri_f": same * (s > t) / GLA_TAU, "stri_b": same * (s < t) / GLA_TAU,
        "mask": np.concatenate([same * (s <= t), same * (s >= t)], 1),
        "add": np.concatenate([np.where(same & (s <= t), 0.0, NEG), np.where(same & (s >= t), 0.0, NEG)], 1),
        "band": np.concatenate([np.where(t >= s, 0.0, NEG), np.zeros((P, P)), np.where(t <= s, 0.0, NEG)], 1),
    }
    perm = np.zeros((P, P))
    for r in range(P):
        if r % 32 < 16:
            perm[r + 16, r] = -1.0
        else:
            perm[r - 16, r] = 1.0
    parts["perm"] = perm
    out = np.zeros((P, CONST_W), np.float32)
    for name, (o, n) in CONST.items():
        out[:, o:o + n] = parts[name]
    return out


def layer1_tables():
    out = np.zeros((P, TABLES_W), np.float32)
    nf = DH // 4
    freqs = (np.float32(10000.0) ** (-np.arange(nf, dtype=np.float32) / np.float32(nf))).astype(np.float32)
    pos = np.arange(LAT)
    for r in range(P):
        where = (pos // GRID_W if r % DH < DH // 2 else pos % GRID_W).astype(np.float32)
        ang = (where * freqs[r % 16]).astype(np.float32)
        out[r, 0:LAT] = np.cos(ang)
        out[r, LAT:2 * LAT] = np.sin(ang)
    for d in range(2):
        for p in range(2):
            o = SEL_AT + (2 * d + p) * P
            for h in range(2):
                out[32 * d + 2 * p + h, o + h * DH:o + (h + 1) * DH] = 1.0
        for h in range(4):
            o = SEL_AT + (4 + d * 4 + h) * P
            out[32 * d + h, o:o + P] = 1.0
    return out


def weight_tiles(w):
    we, wo_e, wod, wo_o, wa = w["w_in_even"][0], w["w_out_even"][0], w["w_in_odd"][0], w["w_out_odd"][0], w["w_ada"]
    order = np.concatenate([np.r_[j * DH:(j + 1) * DH, (4 + j) * DH:(5 + j) * DH] for j in range(4)])
    wo_o = np.concatenate([wo_o[:512], wo_o[512:][order]])

    def spread(src, starts, width):
        out = np.zeros((D, P), np.float32)
        for to, fr in starts:
            out[:, to:to + width] = src[:, fr:fr + width]
        return out

    def columns(kind):
        k = kind[0]
        if k == "ada":
            return wa[kind[1]][:, kind[2] * P:(kind[2] + 1) * P]
        if k == "lr":
            return spread(we, [(0, 1536), (32, 1552)], 16)
        if k == "gates":
            return spread(wod, [(0, 1536), (64, 1540), (32, 1544), (96, 1548)], 4)
        if k in ("gla", "ml"):
            src, p = (we if k == "gla" else wod), kind[1]
            o = {"q": p * P, "k": 256 + p * P, "v0": 512 + 256 * p, "v1": 640 + 256 * p}[kind[2]]
            return src[:, o:o + P]
        if k == "na":
            o = {"q": 1568, "k": 2080, "v": 2592}[kind[2]] + kind[1] * P
            return we[:, o:o + P]
        if k == "sw":
            if kind[2] == "q":
                return wod[:, 1552 + order[kind[1] * P:(kind[1] + 1) * P]]
            o = {"k": 2064, "v": 2192}[kind[2]]
            return wod[:, o:o + P]
        if k == "gate":
            l, f = kind[1], kind[2]
            if f < 4:
                return (wod if l else we)[:, 1024 + f * P:1024 + (f + 1) * P]
            if l == 0:
                return we[:, 3104 + (f - 4) * P:3104 + (f - 3) * P]
            return wod[:, 2320 + order[(f - 4) * P:(f - 3) * P]]
        return (wo_o if kind[1] else wo_e)[:, kind[2] * P:(kind[2] + 1) * P]

    return np.stack([columns(k).reshape(KT, P, P).transpose(1, 0, 2) for k in PLAN])


def bias_tables(rpb):
    q = np.arange(GRID_W)
    start = np.clip(q - 8, 0, GRID_W - 16)
    ok = (q[None, :] >= start[:, None]) & (q[None, :] < start[:, None] + 16)
    dc = np.clip(q[None, :] - q[:, None] + 15, 0, 30)
    out = np.full((8, P, BIAS), NEG, np.float32)
    for half in range(2):
        rows = slice(half * GRID_W, (half + 1) * GRID_W)
        for n, (lo, hi, valid) in enumerate(((1, 15, range(0, 15)), (3, 12, range(3, 11)))):
            for j in range(lo, hi):
                dr = j - half
                if dr not in valid:
                    continue
                o = (FULL_BIAS if n else 0) + (j - lo) * GRID_W
                vals = rpb[:, dr][:, dc]
                out[:, rows, o:o + GRID_W] = np.where(ok[None], vals, np.float32(NEG))
    return out


def layouts(w):
    cols = np.zeros((P, COLS_W), np.float32)

    def put(name, value):
        o, n = COLS[name]
        cols[:, o:o + n] = value

    put("b_ada", w["b_ada"].reshape(2 * 24, P).T)
    put("ln_g", w["ln_g"].reshape(2 * KT, P).T)
    put("ln_b", w["ln_b"].reshape(2 * KT, P).T)
    put("norm_g", np.concatenate([w["gla_norm_g"].reshape(4, P), w["ml_norm_g"].reshape(4, P)]).T)
    put("sink", np.broadcast_to(w["sw_sink"].reshape(1, 8), (P, 8)))
    gb = np.zeros((P, 1), np.float32)
    mb = w["ml_gate_b"].reshape(2, 2, 4)
    for d in range(2):
        gb[32 * d:32 * d + 4, 0] = mb[d, 0]
        gb[64 + 32 * d:64 + 32 * d + 4, 0] = mb[d, 1]
    put("gate_b", gb)
    put("cond", np.stack([w["c"].reshape(KT, P), w["c_ctx"].reshape(KT, P)], 2).transpose(1, 0, 2).reshape(P, 16))
    put("eps", np.array([[LN_EPS, RMS_EPS]], np.float32))
    put("one", 1.0)
    gate_w = np.zeros((P, 512), np.float32)
    for d in range(2):
        gate_w[32 * d:32 * d + 16, d * 256:(d + 1) * 256] = w["gla_gate_w"][0, d]
        gate_w[32 * d + 16, d * 256:(d + 1) * 256] = w["gla_gate_b"][0, d]
    xT = np.concatenate([w["ctx"][0], w["x"][0]]).T.reshape(KT, P, T)
    return {"consts": constants(), "cols": cols, "gate_w": gate_w, "tables": layer1_tables(),
            "bias": bias_tables(w["na_rpb"][0]), "weights": weight_tiles(w), "xT": np.ascontiguousarray(xT)}


def declare(nc, arrays):
    a = {n: nc.dram_tensor(f"in_{n}", v.shape, F32, kind="ExternalInput").ap() for n, v in arrays.items()}
    a["x1T"] = nc.dram_tensor("x1T", (KT, P, T), F32, kind="Internal").ap()
    a["out"] = nc.dram_tensor("out_0", (KT, P, LAT), F32, kind="ExternalOutput").ap()
    return a


def kernel(**inputs):
    from concourse.bacc import Bacc
    from concourse.bass_utils import run_bass_kernel_spmd

    arrays = layouts({k: np.asarray(v) for k, v in inputs.items()})
    counted = None
    for _ in range(2):
        nc = Bacc("TRN2", target_bir_lowering=False, num_devices=1)
        counted = build(nc, declare(nc, arrays), counted)
    r = run_bass_kernel_spmd(nc, [{f"in_{n}": np.ascontiguousarray(v) for n, v in arrays.items()}], core_ids=[0])
    out = r.results[0]["out_0"]
    return np.ascontiguousarray(out.reshape(D, LAT).T).reshape(1, LAT, D)
```

```python
from contextlib import ExitStack

import numpy as np

import concourse.bass as bass
from concourse import mybir

ALU = mybir.AluOpType
ACT = mybir.ActivationFunctionType
F32 = mybir.dt.float32

P = 128
D = 1024
KT = D // P
LAT = 1024
CTX = 256
T = CTX + LAT
NT = T // P
CT = CTX // P
DEPTH = 2
ALPHA = (2.0 * DEPTH) ** 0.25
LN_EPS = 1e-5
RMS_EPS = 1e-6
GLA_TAU = 16.0
CHUNK = 64
GRID_W = 64
ROWS = LAT // GRID_W
DH = 64
QSCALE = DH ** -0.5
NEG = -1e30
LOWEST = -3.0e38
FULL_BIAS = 14 * GRID_W
MID_BIAS = 9 * GRID_W
BIAS = FULL_BIAS + MID_BIAS
VW = 129
GATE_ROWS = 64
WBUFS = 5

CHUNKS_ALL = [(0, CTX), (CTX, 512), (CTX + 512, 512)]
CHUNKS_LAT = CHUNKS_ALL[1:]

CONST = {}
_off = 0
for _name, _w in (("ident", P), ("tri_f", P), ("tri_b", P), ("stri_f", P), ("stri_b", P), ("ones", P),
                  ("mask", 2 * P), ("add", 2 * P), ("perm", P), ("band", 3 * P)):
    CONST[_name] = (_off, _w)
    _off += _w
CONST_W = _off
SEL_AT = 2 * LAT
TABLES_W = SEL_AT + 12 * P
COLS = {}
_off = 0
for _name, _w in (("b_ada", 2 * 24), ("ln_g", 2 * KT), ("ln_b", 2 * KT), ("norm_g", 2 * 4), ("sink", 8), ("gate_b", 1),
                  ("cond", 16), ("eps", 2), ("one", 1)):
    COLS[_name] = (_off, _w)
    _off += _w
COLS_W = _off


def units_even(j):
    out = []
    for t in range(2, NT):
        r = 2 * (t - CT)
        rs = min(max(r - 4, 0), ROWS - 8)
        middle = r >= 4 and r + 1 <= ROWS - 4 and rs == r - 4
        n = (9 if middle else 8) * GRID_W
        off = FULL_BIAS if middle else (rs - r + 7 - 1) * GRID_W
        for hh in range(2):
            out.append((hh, t, CTX + rs * GRID_W, n, off))
    for t in range(CT):
        for hh in range(2):
            out.append((hh, t, 0, 0, 0))
    return out


def units_odd(j):
    out = []
    for t in range(2, NT):
        lo, hi = max(t - 1, 2), min(t + 2, NT)
        for hh in range(2):
            out.append((hh, t, lo * P, (hi - lo) * P, (lo - (t - 1)) * P))
    return out


N_UNITS = (len(units_even(0)), len(units_odd(0)))


def unit_of(uid):
    return (units_even if uid[1] == 0 else units_odd)(uid[2])[uid[3]]


def scan_order(d):
    if d == 0:
        return list(range(NT))
    return list(range(CT - 1, -1, -1)) + list(range(NT - 1, CT - 1, -1))


class Slot:
    pass


def interleave(main, filler):
    out, done, other = [], 0, 0

    def under_way():
        return 0 < done < len(filler) and filler[done][0] == "mm" and filler[done][7] > 0

    for i, s in enumerate(main):
        if s[0] == "lin_turn" and under_way():
            while other and under_way():
                out.append(filler[done])
                done += 1
            other += under_way()
        out.append(s)
        while done < (i + 1) * len(filler) // len(main):
            out.append(filler[done])
            done += 1
            other = other if under_way() else 0
    return out


def project(kind, dest, chunks):
    out = []
    for t0, n in chunks:
        bank, stage = Slot(), Slot()
        out += [("mm", kind, dest, t0, n, bank, stage, part) for part in range(4)]
        if dest in ("v0", "v1", "v", "vv"):
            out.append(("vturn", kind, dest, t0, n, Slot(), stage))
        if dest in ("rq", "kk") and t0 >= CTX:
            out.append(("rope", kind, dest, t0, n, Slot(), stage))
    return out


def attention(l, fills, others):
    units = [(j, i) for j in range(4) for i in range(N_UNITS[l])]
    steps, n, per = [], len(units), N_UNITS[l]

    def named(x):
        j, i = units[x]
        return ("att", l, j, i), unit_of(("att", l, j, i))

    for x in range(-2, n + 2):
        step = []
        if 0 <= x < n:
            step.append(("ptrans", *named(x)))
        if x + 2 < n:
            step += [(kind, *named(x + 2)) for kind in ("scores", "softmax")]
        if 0 <= x - 1 < n:
            step.append(("pv", *named(x - 1)))
        if 0 <= x - 2 < n and units[x - 2][1] % 2:
            step.append(("yout", *named(x - 2)))
        steps.append(step)
    out, at = [], 0
    for j in range(4):
        last = j == 3
        to = len(steps) if last else (j + 1) * per
        out += interleave([s for step in steps[at:to] for s in step], fills[j])
        at = to
        if not last:
            to = (j + 1) * per + 4
            out += interleave([s for step in steps[at:to] for s in step], others[j])
            at = to
    return out


def scan(l, p):
    steps = [dict(l=l, p=p, i=i, t=(scan_order(0)[i], scan_order(1)[i]), wanted=(l == 0 or i >= CT))
             for i in range(NT)]
    for q in steps:
        q["second"] = q["t"][0] in scan_order(1)[:q["i"]]
        assert q["second"] == (q["t"][1] in scan_order(0)[:q["i"]])
    main = []
    for x in range(NT + 4):
        now, one, two, three, four = (steps[x - y] if 0 <= x - y < NT else None for y in range(5))
        turned = four and four["second"] and four["wanted"]
        if three:
            main.append(("lin_inside", three))
        if three:
            main.append(("lin_chunk", three, 0))
        if two:
            main.append(("lin_attend", two))
        if three:
            main.append(("lin_chunk", three, 1))
        if now and l == 0:
            main.append(("lin_gate", now))
        if one:
            main.append(("lin_scale", one))
        if turned:
            main += [("lin_norm", four), ("lin_turn", four, Slot())]
        if three:
            main.append(("lin_out", three))
        if now and l == 0:
            main.append(("lin_log", now))
        if one:
            main.append(("lin_mul", one))
    return main


def ada(l, tiles):
    return [("ada", l, f, Slot()) for f in tiles]


def out_projection(l, part, chunks):
    out = []
    for f in range(KT):
        out += project(("out", l, f, part), "out", chunks)
    return out


def norm(l, ci):
    out = []
    for f in range(KT):
        out += [("centre", l, ci, f), ("spacer",)]
    out += [("square_sum", l, ci), ("rstd", l, ci)]
    for f in range(KT + 1):
        if f < KT:
            out.append(("scale", l, ci, f))
        if f and l == 0:
            out.append(("next", ci, f - 1))
    return out


def qkv(group, j, chunks_q=CHUNKS_ALL):
    out = []
    for w in (("q", "k", "v") if group == "na" else ("q", "k", "v0", "v1")):
        out += project((group, j, w), w, chunks_q if w == "q" else CHUNKS_ALL)
    return out


def between(products, extra):
    ends = [i + 1 for i, s in enumerate(products)
            if s[0] != "mm" and (i + 1 == len(products) or products[i + 1][0] == "mm")
            or s[0] == "mm" and s[7] == 3 and (i + 1 == len(products) or products[i + 1][0] == "mm")]
    out, at, used = [], 0, 0
    for n, e in enumerate(ends):
        out += products[at:e]
        at = e
        while used < (n + 1) * len(extra) // len(ends):
            out.append(extra[used])
            used += 1
    return out


def make_schedule():
    s, early = [("setup",)], project(("lr",), "lr", CHUNKS_ALL)
    for x in range(KT + 1):
        k = x - 1
        if x < KT:
            s += [("ada_row", x), ("ada_row", 8 + x)]
        if x:
            s += [("ada_turn", k), ("ada_turn", 8 + k), ("modulate", k)]
        if x and k % 2:
            s += [early[k // 2], early[4 + k // 2]]
    s += early[8:] + qkv("gla", 0)
    s += interleave(scan(0, 0), qkv("gla", 1))
    s += interleave(scan(0, 1), between(qkv("na", 0), ada(0, range(16, 24))))
    gates = [project(("gate", 0, f), "gate", [c]) for f in range(8) for c in CHUNKS_ALL]
    fills = [between(qkv("na", j + 1), ada(1, range(8 * j, 8 * j + 8))) for j in range(3)] + [sum(gates[9:18], [])]
    s += attention(0, fills, [sum(gates[3 * j:3 * j + 3], []) for j in range(3)])
    s += sum(gates[18:], [])
    s += out_projection(0, 0, CHUNKS_ALL[:2])
    rest = out_projection(0, 1, CHUNKS_ALL[2:])
    s += rest[:7] + [("column_sum", 0, 0), ("column_sum", 0, 1)] + interleave(norm(0, 0) + norm(0, 1), rest[7:])
    ready, rest = [], []
    for kind, dest, chunks in ((("gates",), "gates", CHUNKS_ALL), (("ml", 0, "q"), "q", CHUNKS_LAT),
                               (("ml", 0, "k"), "k", CHUNKS_ALL), (("ml", 0, "v0"), "v0", CHUNKS_ALL)):
        ready += project(kind, dest, chunks[:-1])
        rest += project(kind, dest, chunks[-1:])
        if dest == "gates":
            rest.append(("rows",))
    s += ready[:8] + [("column_sum", 0, 2)] + interleave(norm(0, 2), ready[8:]) + rest
    s += project(("ml", 0, "v1"), "v1", CHUNKS_ALL)
    s += project(("ml", 1, "v0"), "v0", CHUNKS_ALL) + project(("ml", 1, "v1"), "v1", CHUNKS_ALL)
    s += [("rows_exp",)]
    s += [("rows_turn", t, Slot()) for t in range(NT)]
    fill = project(("ml", 1, "q"), "q", CHUNKS_LAT) + project(("ml", 1, "k"), "k", CHUNKS_ALL)
    fill += project(("sw", 0, "k"), "kk", CHUNKS_ALL) + project(("sw", 0, "v"), "vv", CHUNKS_ALL)
    s += interleave(scan(1, 0), fill)
    gates = [project(("gate", 1, f), "gate", [c]) for f in range(8) for c in CHUNKS_LAT]
    rq = [project(("sw", j, "q"), "rq", CHUNKS_LAT) for j in range(4)]
    s += interleave(scan(1, 1), rq[0] + sum(gates[:4], []))
    s += attention(1, [rq[1] + gates[4] + gates[5], gates[7] + rq[2], gates[9] + rq[3], sum(gates[11:14], [])],
                   [gates[6], gates[8], gates[10]])
    s += gates[14] + gates[15]
    s += out_projection(1, 0, CHUNKS_LAT[:1])
    rest = out_projection(1, 1, CHUNKS_LAT[1:])
    s += rest[:7] + [("column_sum", 1, 1)] + interleave(norm(1, 1), rest[7:])
    s += [("column_sum", 1, 2)] + norm(1, 2)
    banks, stages, out = {}, {}, []
    for st in s:
        st = list(st)
        at = {"mm": 5, "vturn": 5, "rope": 5, "ada": 3, "lin_turn": 2, "rows_turn": 2}.get(st[0])
        if at is not None:
            st[at] = banks.setdefault(st[at], len(banks))
        if st[0] in ("mm", "vturn", "rope"):
            staged = st[2] in ("v0", "v1", "v", "vv", "gate") or (st[2] in ("rq", "kk") and st[3] >= CTX)
            st[6] = stages.setdefault(st[6], len(stages)) if staged else None
        out.append(tuple(st))
    return out


SCHEDULE = make_schedule()
PLAN = []
for _s in SCHEDULE:
    _k = ("ada", 0, _s[1]) if _s[0] == "ada_row" else ("ada", _s[1], _s[2]) if _s[0] == "ada" else _s[1] if _s[0] == "mm" else None
    if _k not in (None, ("lr",)) and _k not in PLAN:
        PLAN.append(_k)
WEIGHT_AT = {k: n for n, k in enumerate(PLAN)}
LAST_CHUNK = {s[1]: s[3] for s in SCHEDULE if s[0] == "mm"}
RESID = [s for s in SCHEDULE if s[0] == "mm" and s[2] == "out" and s[7] == 0]
RESID_AT = {(s[1][1], s[1][2], s[3]): i for i, s in enumerate(RESID)}
STAGED = {s[6]: s for s in SCHEDULE if s[0] == "mm" and s[7] == 0 and s[6] is not None}


def pair_slot(kind):
    order = [("gla", 0), ("gla", 1), ("na", 0), ("na", 1), ("na", 2), ("na", 3), ("ml", 0), ("ml", 1),
             ("sw", 0), ("sw", 1), ("sw", 2), ("sw", 3)]
    n = order.index(kind[:2])
    return n % 2, (order[n - 2] if n >= 2 else None)


def readers(pair):
    if pair[0] in ("gla", "ml"):
        return [("lin_pe", pair[0] == "ml", pair[1]), ("lin_dve", pair[0] == "ml", pair[1])]
    return [("att_pe", int(pair[0] == "sw"), pair[1])]


def key_chunks(unit):
    hh, t, k0, nk, _o = unit
    full = [(o, P, (k0 + o) // P) for o in range(0, nk - nk % P, P)]
    ctx = [(nk + o, P, o // P) for o in range(0, CTX, P)]
    part = [(nk - nk % P, nk % P, (k0 + nk - nk % P) // P)] if nk % P else []
    return full + ctx + part


def before(uid, n=1):
    _, l, j, i = uid
    i += j * N_UNITS[l] - n
    return None if i < 0 else ("att", l, i // N_UNITS[l], i % N_UNITS[l])


class Counts:

    def __init__(self, known, sems):
        self.known, self.sems, self.now, self.new = known, sems, {}, {}

    def up(self, name, *keys, by=1):
        self.now[name] = self.now.get(name, 0) + by
        for key in keys:
            assert key not in self.new, key
            self.new[key] = (name, self.now[name])
        return self.sems[name], by

    def at(self, key):
        name, value = self.known[key] if self.known is not None else ("vector_done", 1)
        return self.sems[name], value

    def last(self, name):
        return self.sems[name], self.now[name]


SEMS = (["pool_done", "tensor_done", "vector_done", "scalar_done", "constants_loaded", "lr_loaded", "tables_loaded", 
         "residual_loaded0", "residual_loaded1", "bias_loaded0", "bias_loaded1"]
        + ["spilled0", "spilled1", "spilled2", "stored1", "stored2"] + [f"x_loaded{k}" for k in range(KT)] + [f"weight_loaded{i}" for i in range(WBUFS)])


def build(nc, a, known):
    with ExitStack() as stack:
        def sb(name, shape):
            return stack.enter_context(nc.sbuf_tensor(name, shape, F32))

        def bank(name, n=1):
            return stack.enter_context(nc.psum_tensor(name, [P, n * 512], F32))

        sems = {n: stack.enter_context(nc.semaphore(n)) for n in SEMS}
        c = Counts(known, sems)
        at, up = c.at, c.up

        hT = sb("hT", [P, KT, T])
        yT = sb("yT", [P, KT, T])
        weights = sb("weights", [P, WBUFS, KT, P])
        pair = sb("pair", [P, 2, 2 * T + NT * 2 * VW])
        kvT = sb("kvT", [P, T])
        kvV = sb("kvV", [P, NT, P])
        consts = sb("consts", [P, CONST_W])
        tables = sb("tables", [P, TABLES_W])
        cols = sb("cols", [P, COLS_W])
        mods = sb("mods", [P, 2, 24, 2])
        vstage = sb("vstage", [P, 2, 512])
        work = sb("work", [P, 4100])
        gate_w = sb("gate_w", [P, 512])
        tokc = sb("tokc", [P, NT, 3, 8])
        rows2 = sb("rows2", [GATE_ROWS, 2, T])
        rowm = sb("rowm", [GATE_ROWS, T // CHUNK])
        stat = sb("stat", [P, 4, 8])
        rstat = sb("rstat", [P, 16])

        PJ = [bank("proj0"), bank("proj1")]
        SC = bank("scores", 2)
        TP = [bank("turned0"), bank("turned1")]
        OV = bank("values")
        MI = bank("misc")

        def const(name):
            o, n = CONST[name]
            return consts[:, o:o + n]

        def col(name, i, n=1):
            o = COLS[name][0] + i
            return cols[:, o:o + n]

        ident = const("ident")

        def pq(slot):
            return pair[:, slot, 0:T]

        def pk(slot):
            return pair[:, slot, T:2 * T]

        def pv(slot):
            return pair[:, slot, 2 * T:].rearrange("p (t h w) -> p t h w", t=NT, h=2)

        def lin_slot(l, p):
            return pair_slot(("ml" if l else "gla", p))[0]

        def att_slot(l, j):
            return pair_slot(("sw" if l else "na", j))[0]

        prob = [work[:, 0:832], work[:, 832:1664]]
        prob_t = [work[:, 1664:1664 + 896], work[:, 2560:2560 + 896]]
        ytok = work[:, 3456:3584]
        LIN = ({"g": 0, "na": 2, "eb0": 4, "eb1": 6, "enb": 8, "ekd": 10, "kin": 12, "kd": 14, "qin": 18, "at": 22},
               {"eb0": 0, "eb1": 2, "w": 4, "qz": 8, "kd": 14, "qin": 18, "at": 22})

        def lin(l, name, n=2):
            o = LIN[l][name] * P
            return work[:, o:o + n * P]

        def buf(q, name):
            o = {"kd": (4, 0), "qin": (4, 512), "at": (5, 0), "qz": (5, 512)}[name]
            return yT[:, o[0], o[1]:o[1] + 512] if q["i"] % 2 else lin(q["l"], name, 4)

        def decays(q):
            n = (q["p"] * NT + q["i"]) % 3
            return yT[:, 4, 1024:1280] if n == 2 else lin(q["l"], f"eb{n}")

        squares = yT[:, 5, 1024:1152]

        def tiles(ap):
            return ap.rearrange("p (x n) -> p x n", n=P)

        state = [work[:, 26 * P + d * VW:26 * P + (d + 1) * VW] for d in range(2)]
        osum = work[:, 26 * P + 2 * VW:26 * P + 2 * VW + 512]
        x_stage = [work[:, 0:512], work[:, 512:1024]]
        sq_stage = [work[:, 1024:1536], work[:, 1536:2048]]
        mean_neg, rstd = work[:, 2048:2560], work[:, 2560:3072]

        def two(ap):
            return ap.rearrange("p (h n) -> p h n", h=2)

        def by_dir(ap):
            return ap.rearrange("p (d h n) -> p d h n", d=2, h=2)

        def over_heads(ap):
            return two(ap).unsqueeze(2).broadcast_to([P, 2, 2, P])

        def y_block(p, t):
            return yT[:, 2 * p:2 * p + 2, t * P:(t + 1) * P]

        def chunk_no(t0):
            return [x[0] for x in CHUNKS_ALL].index(t0)

        def sum_bank(t0):
            return [SC[:, 0:512], SC[:, 512:1024], TP[0][:, :]][chunk_no(t0)]

        def ada_order(f):
            return 2 * (f % 8) + f // 8

        def ada_feature(n):
            return n // 2 + n % 2 * 8

        def ada_bank(f):
            return (MI[:, :], OV[:, :], TP[0][:, :], TP[1][:, :], SC[:, 0:512], SC[:, 512:1024])[ada_order(f) % 6]

        def ada_row(f):
            return rows2[0:2, f // 8, f % 8 * P:(f % 8 + 1) * P]

        def total(t0, n):
            return kvV[:, :, :].rearrange("p t n -> p (t n)")[:, t0:t0 + n]

        def tail(l, ci):
            return (l, ci) == (1, 2)

        def square_bank(ci):
            return [MI, OV, TP[1]][ci]

        def step_before(q, first=0, by=1):
            n = q["p"] * (NT - first) + q["i"] - first - by
            return None if n < 0 else (q["l"], n // (NT - first), n % (NT - first) + first)

        def first_wanted(l):
            return CT if l else 0

        def out_bank(l, d):
            if l:
                return (OV[:, 0:2 * VW], SC[:, 512:512 + 2 * VW])[d]
            return OV[:, d * 2 * P:(d + 1) * 2 * P]

        block = stack.enter_context(nc.Block())

        @block.sync
        def _(sp):
            for name, dst in (("consts", consts), ("cols", cols), ("gate_w", gate_w)):
                sp.dma_start(dst[:, :], a[name]).then_inc(*up("constants_loaded", ("loaded", name), by=16))
            sent = [0, 0]

            def load_weights(upto):
                while sent[0] < min(upto, len(PLAN)):
                    n = sent[0]
                    if n >= WBUFS:
                        sp.wait_ge(*at(("weight_used", n - WBUFS)))
                    sp.dma_start(weights[:, n % WBUFS, :, :], a["weights"][n]).then_inc(
                        *up(f"weight_loaded{n % WBUFS}", ("weight", n), by=16))
                    sent[0] += 1

            def load_bias(j, hh):
                if j >= 1:
                    sp.wait_ge(*at(("softmax_dve", ("att", 0, j - 1, 14 + hh))))
                sp.dma_start(tables[:, hh * BIAS:(hh + 1) * BIAS], a["bias"][2 * j + hh]).then_inc(
                    *up(f"bias_loaded{hh}", ("bias", j, hh), by=16))

            def load_x(k):
                if k < KT:
                    sp.dma_start(hT[:, k, :], a["xT"][k]).then_inc(*up(f"x_loaded{k}", ("x", k), by=16))

            load_weights(2)
            load_x(0)
            load_weights(WBUFS)
            sp.dma_start(vstage[:, :, :].rearrange("p a b -> p (a b)"),
                         a["weights"][len(PLAN)].rearrange("p k n -> p (k n)")).then_inc(
                *up("lr_loaded", ("lr_loaded",), by=16))
            load_x(1)
            for s in SCHEDULE:
                if s[0] == "modulate":
                    load_x(s[1] + 2)
                if s[0] == "ada":
                    load_weights(WEIGHT_AT[("ada", s[1], s[2])] + WBUFS)
                if s[0] == "ada_row":
                    load_weights(WEIGHT_AT[("ada", 0, s[1])] + WBUFS)
                if s[0] == "mm" and s[7] == 0:
                    if s[2] == "out":
                        l, f, t0, n, i = s[1][1], s[1][2], s[3], s[4], sent[1]
                        if i >= 2:
                            sp.wait_ge(*at(("resid_used", i - 2)))
                        if f == 0 and t0 == (CTX if l else 0):
                            sp.wait_ge(*at(("att_pe", l, 3)))
                            sp.wait_ge(*at(("y_turned_pe", l, 3)))
                            if l:
                                for ci in range(1, 3):
                                    sp.wait_ge(*at(("spill", ci)))
                        src = a["x1T"] if l else a["xT"]
                        sp.dma_start(x_stage[i % 2][:, 0:n], src[f, :, t0:t0 + n]).then_inc(
                            *up(f"residual_loaded{i % 2}", ("resid", i), by=16))
                        sent[1] += 1
                    if s[2] != "lr":
                        load_weights(WEIGHT_AT[s[1]] + WBUFS)
                if s[0] == "lin_scale" and s[1]["l"] == 0 and s[1]["p"] == 1 and s[1]["i"] < 2:
                    load_bias(0, s[1]["i"])
                if s[0] == "scores" and s[1][1] == 0 and s[1][2] < 3 and s[1][3] in (16, 17):
                    load_bias(s[1][2] + 1, s[1][3] - 16)
                if s[0] == "centre" and s[1:] == (0, 0, 0):
                    sp.wait_ge(*at(("softmax_dve", ("att", 0, 3, 15))))
                    sp.dma_start(tables[:, :], a["tables"]).then_inc(*up("tables_loaded", ("tables",), by=16))
            for ci in range(3):
                sp.wait_ge(*at(("spill", ci)))
            sp.wait_ge(*at(("stored", 1)))
            sp.wait_ge(*at(("stored", 2)))

        @block.tensor
        def _(pe):
            def done(ins, *keys):
                ins.then_inc(*up("tensor_done", *keys))

            def s_setup():
                pe.wait_ge(*at(("cond",)))

            def s_ada(l, f, u):
                n = WEIGHT_AT[("ada", l, f)]
                pe.wait_ge(*at(("weight", n)))
                pe.wait_ge(*at(("proj_free", u - 2)))
                for k in range(KT):
                    last = nc.tensor.matmul(PJ[u % 2][:, 0:2], weights[:, n % WBUFS, k, :], col("cond", 2 * k, 2),
                                            start=(k == 0), stop=(k == KT - 1))
                done(last, ("ada", l, f), ("weight_used", n))

            def s_ada_row(f):
                n = WEIGHT_AT[("ada", 0, f)]
                pe.wait_ge(*at(("weight", n)))
                if ada_order(f) >= 6:
                    pe.wait_ge(*at(("mods", 0, ada_feature(ada_order(f) - 6))))
                for k in range(KT):
                    last = nc.tensor.matmul(ada_bank(f)[0:2, 0:P], col("cond", 2 * k, 2), weights[:, n % WBUFS, k, :],
                                            start=(k == 0), stop=(k == KT - 1))
                done(last, ("ada_row", f), ("weight_used", n))

            def s_ada_turn(f):
                pe.wait_ge(*at(("row_copied", f)))
                done(nc.tensor.transpose(ada_bank(f)[:, P:P + 2], ada_row(f), ident[0:2, 0:2]), ("ada_turn", f))

            def s_column_sum(l, ci):
                t0, n = CHUNKS_ALL[ci]
                pe.wait_ge(*at(("total", l, KT - 1, t0)))
                done(nc.tensor.matmul(sum_bank(t0)[:, 0:n], const("ones"), total(t0, n), start=True, stop=True,
                                      skip_group_check=True), ("sum", l, t0))

            def s_mm(kind, dest, t0, n, u, stage, part):
                w = WEIGHT_AT.get(kind)
                src = yT if dest == "out" else hT
                if part == 0:
                    pe.wait_ge(*at(("lr_loaded",) if dest == "lr" else ("weight", w)))
                    if u >= 2:
                        pe.wait_ge(*at(("proj_free", u - 2)))
                    if dest == "gates":
                        pe.wait_ge(*at(("h1", chunk_no(t0))))
                    if dest == "out" and kind[2] == 0:
                        for f in range(KT):
                            pe.wait_ge(*at(("gated", kind[1], f, t0)))
                for k in range(2 * part, 2 * part + 2):
                    if dest == "lr" and t0 <= CTX:
                        pe.wait_ge(*at(("modulated", k)))
                    tile = (vstage[:, k // 4, k % 4 * P:(k % 4 + 1) * P] if dest == "lr" else
                            weights[:, w % WBUFS, k, :])
                    last = nc.tensor.matmul(PJ[u % 2][:, 0:n], tile, src[:, k, t0:t0 + n],
                                            start=(k == 0), stop=(k == KT - 1))
                if part == 3:
                    done(last, ("proj", u), *([("weight_used", "lr" if dest == "lr" else w)] if LAST_CHUNK[kind] == t0 else []))

            def s_centre(l, ci, f):
                if not tail(l, ci):
                    return
                t0, n = CHUNKS_ALL[ci]
                pe.wait_ge(*at(("square", l, ci, f)))
                done(nc.tensor.matmul(square_bank(ci)[:, 0:n], const("ones"), total(t0, n) if f == 0 else
                                      sq_stage[f % 2][:, 0:n], start=(f == 0), stop=(f == KT - 1),
                                      skip_group_check=True),
                     ("square_used", l, ci, f), *([("square_sum", l, ci)] if f == KT - 1 else []))

            def s_square_sum(l, ci):
                if tail(l, ci):
                    return
                t0, n = CHUNKS_ALL[ci]
                pe.wait_ge(*at(("square_used", l, ci, KT - 1)))
                done(nc.tensor.matmul(square_bank(ci)[:, 0:n], const("ones"), total(t0, n), start=True, stop=True,
                                      skip_group_check=True), ("square_sum", l, ci))

            def s_vturn(kind, dest, t0, n, u, stage):
                pe.wait_ge(*at(("staged", stage)))
                pe.wait_ge(*at(("proj_free", u - 2)))
                for i in range(n // P):
                    last = nc.tensor.transpose(PJ[u % 2][:, i * P:(i + 1) * P],
                                               vstage[:, stage % 2, i * P:(i + 1) * P], ident)
                done(last, ("proj", u), ("stage_used", stage))

            def s_rope(kind, dest, t0, n, u, stage):
                pe.wait_ge(*at(("staged", stage)))
                pe.wait_ge(*at(("proj_free", u - 2)))
                done(nc.tensor.matmul(PJ[u % 2][:, 0:n], const("perm"), vstage[:, stage % 2, 0:n], start=True,
                                      stop=True), ("proj", u))

            def s_scores(uid, unit):
                _, l, j, i = uid
                hh, t, k0, nk, _o = unit
                if i == 0:
                    for w in (("rq",) if l else ("q", "k", "v")):
                        pe.wait_ge(*at(("filled", "sw" if l else "na", j, w)))
                    if l:
                        pe.wait_ge(*at(("filled", "sw", 0, "kk")))
                        pe.wait_ge(*at(("filled", "sw", 0, "vv")))
                    if j == 0:
                        pe.wait_ge(*at(("lin_dve", l, 1)))
                        pe.wait_ge(*at(("lin_act", l, 1)))
                if before(uid):
                    pe.wait_ge(*at(("softmax_dve", before(uid))))
                lo, hi = hh * DH, hh * DH + DH
                q = pq(att_slot(l, j))[lo:hi, t * P:(t + 1) * P]
                keys = kvT[:, :] if l else pk(att_slot(l, j))
                for o in range(0, nk, 512):
                    w = min(512, nk - o)
                    nc.tensor.matmul(SC[:, o:o + w], q, keys[lo:hi, k0 + o:k0 + o + w], start=True, stop=True)
                co = max(512, nk)
                done(nc.tensor.matmul(SC[:, co:co + CTX], q, keys[lo:hi, 0:CTX], start=True, stop=True,
                                      skip_group_check=True), ("scores", uid))

            def s_ptrans(uid, unit):
                pe.wait_ge(*at(("softmax_act", uid)))
                if before(uid):
                    pe.wait_ge(*at(("pt", before(uid), 0)))
                    if len(key_chunks(unit_of(before(uid)))) > 4:
                        pe.wait_ge(*at(("pt", before(uid), 1)))
                    elif before(uid, 2) and len(key_chunks(unit_of(before(uid, 2)))) > 4:
                        pe.wait_ge(*at(("pt", before(uid, 2), 1)))
                chunks = key_chunks(unit)
                for x, (o, w, _t) in enumerate(chunks):
                    last = nc.tensor.transpose(TP[x // 4][0:w, (x % 4) * P:(x % 4 + 1) * P],
                                               prob[uid[3] % 2][:, o:o + w], ident)
                    if x % 4 == 3 or x == len(chunks) - 1:
                        done(last, ("turned", uid, x // 4), *([("turned", uid)] if x == len(chunks) - 1 else []))

            def s_pv(uid, unit):
                _, l, j, i = uid
                hh = unit[0]
                vals = kvV[:, :, :] if l else pv(att_slot(l, j))[:, :, 0, 0:P]
                chunks = key_chunks(unit)
                if before(uid):
                    pe.wait_ge(*at(("att_out", before(uid))))
                for x, (o, w, t) in enumerate(chunks):
                    if x % 4 == 0:
                        pe.wait_ge(*at(("pt", uid, x // 4)))
                    last = nc.tensor.matmul(OV[:, 0:DH], prob_t[i % 2][0:w, x * P:(x + 1) * P],
                                            vals[0:w, t, hh * DH:(hh + 1) * DH], start=(x == 0),
                                            stop=(x == len(chunks) - 1))
                done(last, ("pv", uid), *([("att_pe", l, j)] if i == N_UNITS[l] - 1 else []))

            def s_yout(uid, unit):
                _, l, j, i = uid
                pe.wait_ge(*at(("att_out", uid)))
                if before(uid, 2):
                    pe.wait_ge(*at(("y_copied", before(uid, 2))))
                done(nc.tensor.transpose(MI[:, 0:P], ytok, ident), ("ytok_used", uid),
                     *([("y_turned_pe", l, j)] if i == N_UNITS[l] - 1 else []))

            def s_lin_gate(q):
                p, i = q["p"], q["i"]
                if i == 0:
                    pe.wait_ge(*at(("filled_lr",)))
                    pe.wait_ge(*at(("loaded", "gate_w")))
                if step_before(q):
                    pe.wait_ge(*at(("g", *step_before(q))))
                for d in range(2):
                    r, o, t = slice(32 * d, 32 * d + 17), d * 256 + p * P, q["t"][d]
                    if d:
                        pe.wait_ge(*c.last("tensor_done"))
                    done(nc.tensor.matmul(SC[:, d * P:(d + 1) * P], kvT[r, t * P:(t + 1) * P], gate_w[r, o:o + P],
                                          start=True, stop=True), ("gate", p, i, d))

            def s_lin_scale(q):
                l, p, i = q["l"], q["p"], q["i"]
                if i == 0:
                    for w in ("q", "k", "v0", "v1"):
                        pe.wait_ge(*at(("filled", "ml" if l else "gla", p, w)))
                    if l:
                        pe.wait_ge(*at(("rows_turned", NT - 1)))
                        pe.wait_ge(*at(("tables",)))
                if step_before(q):
                    pe.wait_ge(*at(("scale_act", *step_before(q))))
                    pe.wait_ge(*at(("scale_done", *step_before(q))))
                if l == 0:
                    pe.wait_ge(*at(("g", l, p, i)))
                for d in range(2):
                    cs = slice(q["t"][d] * P, (q["t"][d] + 1) * P)
                    if l == 0:
                        g = lin(0, "g")[:, d * P:(d + 1) * P]
                        nc.tensor.matmul(SC[:, 512 + d * P:640 + d * P], g, const("tri_" + "fb"[d]), start=True,
                                         stop=True)
                        nc.tensor.matmul(SC[:, 768 + d * P:896 + d * P], const("stri_" + "fb"[d]), g, start=True,
                                         stop=True)
                    elif q["wanted"]:
                        for h in range(2):
                            o = SEL_AT + (4 + d * 4 + 2 * p + h) * P
                            last = nc.tensor.matmul(SC[:, (2 * d + h) * P:(2 * d + h + 1) * P],
                                                    tables[0:GATE_ROWS, o:o + P], rows2[:, 0, cs], start=True,
                                                    stop=True)
                        if d:
                            done(last, ("spread", p, i))
                for d in range(2):
                    cs = slice(q["t"][d] * P, (q["t"][d] + 1) * P)
                    if l:
                        o = SEL_AT + (2 * d + p) * P
                        nc.tensor.matmul(MI[:, 256 + d * P:384 + d * P], tables[0:GATE_ROWS, o:o + P],
                                         rows2[:, 1, cs], start=True, stop=True)
                    last = nc.tensor.transpose(MI[:, d * P:(d + 1) * P], pk(lin_slot(l, p))[:, cs], ident)
                done(last, ("scale", l, p, i))

            def s_lin_attend(q):
                if not q["wanted"]:
                    return
                l, p, i = q["l"], q["p"], q["i"]
                pe.wait_ge(*at(("scale_done", l, p, i)))
                if step_before(q, first_wanted(l)):
                    pe.wait_ge(*at(("attend_done", *step_before(q, first_wanted(l)))))
                if l:
                    pe.wait_ge(*at(("q_padded", p, i)))
                for d in range(2):
                    t = q["t"][d]
                    keys = pk(lin_slot(l, p))[:, t * P:(t + 1) * P] if l else lin(0, "kin")[:, d * P:(d + 1) * P]
                    last = nc.tensor.matmul(TP[0][:, 2 * d * P:2 * (d + 1) * P], keys,
                                            buf(q, "qz" if l else "qin")[:, 2 * d * P:2 * (d + 1) * P],
                                            start=True, stop=True)
                done(last, ("attend", l, p, i))

            def s_lin_inside(q):
                if not q["wanted"]:
                    return
                l, p, i = q["l"], q["p"], q["i"]
                vw = VW if l else P
                pe.wait_ge(*at(("attend_done", l, p, i)))
                if step_before(q, first_wanted(l)):
                    pe.wait_ge(*at(("lin_read", *step_before(q, first_wanted(l)))))
                for d in range(2):
                    for h in range(2):
                        o = (2 * d + h) * P
                        last = nc.tensor.matmul(out_bank(l, d)[:, h * vw:(h + 1) * vw], buf(q, "at")[:, o:o + P],
                                                pv(lin_slot(l, p))[:, q["t"][d], h, 0:vw],
                                                start=(h == 0 and (l == 1 or d == 0)), stop=False,
                                                skip_group_check=True)
                done(last, ("inside", l, p, i))

            def s_lin_chunk(q, n):
                l, p, i = q["l"], q["p"], q["i"]
                slot, vw = lin_slot(l, p), (VW if l else P)
                if n == 0:
                    pe.wait_ge(*at(("scale_done", l, p, i)))
                for d in range(2):
                    if n == 0 and i == 0:
                        pe.wait_ge(*at(("state0", l, p)))
                    else:
                        pe.wait_ge(*at(("state", l, p, *((i, 0) if n else (i - 1, 1)), d)))
                    half = n if d == 0 else 1 - n
                    r = slice(half * CHUNK, (half + 1) * CHUNK)
                    for h in range(2) if q["wanted"] else ():
                        queries = buf(q, "qin")[:, (2 * d + h) * P:(2 * d + h + 1) * P][:, r]
                        last = nc.tensor.matmul(out_bank(l, d)[r, h * vw:(h + 1) * vw], queries, state[d][:, 0:vw],
                                                start=False, stop=(n == 1), skip_group_check=True)
                    if q["wanted"]:
                        end = (i, n, d) == (NT - 1, 1, 1)
                        done(last, ("lin_o", l, p, i, n, d), *([("lin_pe", bool(l), p)] if end else []))
                if i == NT - 1 and n == 1:
                    return
                if i == 0 and n == 0 and p:
                    pe.wait_ge(*at(("state", l, 0, NT - 1, 0, 1)))
                for d in range(2):
                    half = n if d == 0 else 1 - n
                    for h in range(2):
                        o = (2 * half + d) * P + h * DH
                        last = nc.tensor.matmul(TP[1][h * DH:(h + 1) * DH, d * vw:(d + 1) * vw],
                                                buf(q, "kd")[:, o:o + DH], pv(slot)[:, q["t"][d], h, 0:vw],
                                                start=True, stop=True, skip_group_check=True)
                done(last, ("update", l, p, i, n))

            def s_lin_turn(q, u):
                l, p, i = q["l"], q["p"], q["i"]
                pe.wait_ge(*at(("lin_y", l, p, i)))
                pe.wait_ge(*at(("proj_free", u - 2)))
                first = 0 if q["t"][0] < q["t"][1] else 1
                for h in range(2):
                    for x in range(2):
                        d = first if x == 0 else 1 - first
                        last = nc.tensor.transpose(PJ[u % 2][:, (2 * h + x) * P:(2 * h + x + 1) * P],
                                                   osum[:, (2 * d + h) * P:(2 * d + h + 1) * P], ident)
                done(last, ("proj", u), ("osum_used", l, p, i))

            def s_rows_turn(t, u):
                if t == 0:
                    pe.wait_ge(*at(("rows_act",)))
                    pe.wait_ge(*at(("rows_dve",)))
                pe.wait_ge(*at(("proj_free", u - 2)))
                for i, k in enumerate((0, 6, 7)):
                    last = nc.tensor.transpose(PJ[u % 2][:, i * GATE_ROWS:(i + 1) * GATE_ROWS],
                                               yT[0:GATE_ROWS, k, t * P:(t + 1) * P],
                                               ident[0:GATE_ROWS, 0:GATE_ROWS])
                done(last, ("proj", u))

            part = {"setup": s_setup, "ada": s_ada, "ada_row": s_ada_row, "ada_turn": s_ada_turn,
                    "mm": s_mm, "vturn": s_vturn, "rope": s_rope, "scores": s_scores,
                    "ptrans": s_ptrans, "pv": s_pv, "yout": s_yout, "lin_gate": s_lin_gate,
                    "lin_scale": s_lin_scale, "lin_attend": s_lin_attend,
                    "lin_inside": s_lin_inside, "lin_chunk": s_lin_chunk, "lin_turn": s_lin_turn, "rows_turn": s_rows_turn,
                    "column_sum": s_column_sum, "centre": s_centre, "square_sum": s_square_sum}
            for s in SCHEDULE:
                if s[0] in part:
                    part[s[0]](*s[1:])

        @block.vector
        def _(dve):
            V = nc.vector

            def link(ins, *keys):
                ins.then_inc(*up("vector_done", *keys))
                dve.wait_ge(*c.last("vector_done"))

            def s_setup():
                link(V.memset(kvT[:, :], 1.0), ("lr_ones",))
                for slot in range(2):
                    link(V.memset(pv(slot)[:, :, :, P:VW], 1.0), ("v_ones", slot))
                dve.wait_ge(*at(("cond_exp",)))
                cond = col("cond", 0, 16)
                link(V.tensor_scalar(rstat[:, :], rstat[:, :], 1.0, None, ALU.add))
                link(V.reciprocal(rstat[:, :], rstat[:, :]))
                link(V.tensor_tensor(cond, cond, rstat[:, :], ALU.mult), ("cond",))

            def s_ada(l, f, u):
                dve.wait_ge(*at(("ada", l, f)))
                link(V.tensor_scalar(mods[:, l, f, :], PJ[u % 2][:, 0:2], col("b_ada", l * 24 + f),
                                     1.0 if 8 <= f < 16 else 0.0, ALU.add, ALU.add), ("mods", l, f), ("proj_free", u))

            def s_ada_row(f):
                dve.wait_ge(*at(("ada_row", f)))
                link(V.tensor_copy(ada_row(f), ada_bank(f)[0:2, 0:P]), ("row_copied", f))

            def s_ada_turn(f):
                dve.wait_ge(*at(("ada_turn", f)))
                link(V.tensor_scalar(mods[:, 0, f, :], ada_bank(f)[:, P:P + 2], col("b_ada", f),
                                     1.0 if 8 <= f < 16 else 0.0, ALU.add, ALU.add), ("mods", 0, f))

            def s_modulate(k):
                dve.wait_ge(*at(("x", k)))
                for w, (t0, n) in ((1, (0, CTX)), (0, (CTX, LAT))):
                    link(V.tensor_scalar(hT[:, k, t0:t0 + n], hT[:, k, t0:t0 + n], mods[:, 0, 8 + k, w:w + 1],
                                         mods[:, 0, k, w:w + 1], ALU.mult, ALU.add),
                         *([] if w else [("modulated", k)]))

            def s_mm(kind, dest, t0, n, u, stage, part):
                if part != 3:
                    return
                ps = PJ[u % 2][:, 0:n]
                if dest == "gate":
                    l, f = kind[1], kind[2]
                    e, y = vstage[:, stage % 2, 0:n], yT[:, f, t0:t0 + n]
                    dve.wait_ge(*at(("y_turned", l, f)))
                    dve.wait_ge(*at(("staged", stage)))
                    link(V.tensor_tensor(y, y, ps, ALU.mult), ("proj_free", u))
                    link(V.tensor_scalar(e, e, 1.0, None, ALU.add))
                    link(V.reciprocal(e, e))
                    link(V.tensor_tensor(y, y, e, ALU.mult), ("gated", l, f, t0), ("stage_used", stage))
                elif dest == "out":
                    l, f = kind[1], kind[2]
                    i = RESID_AT[(l, f, t0)]
                    dve.wait_ge(*at(("proj", u)))
                    dve.wait_ge(*at(("resid_scaled", i)))
                    w = 1 if t0 == 0 else 0
                    link(V.scalar_tensor_tensor(out=hT[:, f, t0:t0 + n], in0=ps, scalar=mods[:, l, 16 + f, w:w + 1],
                                                in1=x_stage[i % 2][:, 0:n], op0=ALU.mult, op1=ALU.add),
                         ("proj_free", u), ("resid_sum", l, f, t0), ("resid_used", i))

            def s_vturn(kind, dest, t0, n, u, stage):
                if kind[0] == "ml":
                    return
                dve.wait_ge(*at(("proj", u)))
                nt, t = n // P, t0 // P
                ps = PJ[u % 2][:, 0:n].rearrange("p (t n) -> p t n", n=P)
                if dest == "vv":
                    dst = kvV[:, t:t + nt, :]
                    keys = [("filled", "sw", 0, "vv")]
                else:
                    slot, prev = pair_slot(kind)
                    for r in readers(prev) if prev and t0 == 0 else []:
                        dve.wait_ge(*at(r))
                    dst = pv(slot)[:, t:t + nt, 1 if dest == "v1" else 0, 0:P]
                    keys = [("filled", kind[0], kind[1], dest)]
                link(V.tensor_copy(dst, ps), ("proj_free", u), *(keys if t0 + n == T else []))

            def s_rope(kind, dest, t0, n, u, stage):
                dve.wait_ge(*at(("proj", u)))
                if kind == ("sw", 0, "k") and t0 == CTX:
                    dve.wait_ge(*at(("tables",)))
                st = vstage[:, stage % 2, 0:n]
                ps = PJ[u % 2][:, 0:n]
                if dest == "kk":
                    dst, key = kvT[:, t0:t0 + n], ("filled", "sw", 0, "kk")
                else:
                    slot, prev = pair_slot(kind)
                    for r in readers(prev) if t0 == CTX else []:
                        dve.wait_ge(*at(r))
                    dst, key = pq(slot)[:, t0:t0 + n], ("filled", "sw", kind[1], "rq")
                lo = t0 - CTX
                link(V.tensor_tensor(dst, ps, tables[:, LAT + lo:LAT + lo + n], ALU.mult), ("proj_free", u))
                link(V.tensor_tensor(st, st, tables[:, lo:lo + n], ALU.mult))
                link(V.tensor_tensor(dst, dst, st, ALU.add), ("stage_used", stage), *([key] if t0 + n == T else []))

            def s_softmax(uid, unit):
                _, l, j, i = uid
                hh, t, k0, nk, bo = unit
                st = stat[:, i % 4, :]
                dve.wait_ge(*at(("scores", uid)))
                if before(uid, 2):
                    dve.wait_ge(*at(("turned", before(uid, 2))))
                if l == 0 and i < 2:
                    dve.wait_ge(*at(("bias", j, hh)))
                co = max(512, nk)
                link(V.tensor_scalar(prob[i % 2][:, nk:nk + CTX], SC[:, co:co + CTX], 0.0, None, ALU.add, ALU.max,
                                     accum_out=st[:, 1:2]))
                if nk:
                    bias = const("band")[:, bo:bo + nk] if l else tables[:, hh * BIAS + bo:hh * BIAS + bo + nk]
                    link(V.tensor_tensor_reduce(prob[i % 2][:, 0:nk], SC[:, 0:nk], bias, 1.0, LOWEST, ALU.add,
                                                ALU.max, st[:, 0:1]))
                if l:
                    link(V.tensor_scalar(st[:, 0:1], st[:, 0:1], col("sink", j + 4 * hh), None, ALU.max))
                link(V.tensor_scalar(st[:, 2:3], st[:, 1:2], st[:, 0:1] if nk else LOWEST, -1.0, ALU.max, ALU.mult),
                     ("softmax_dve", uid))

            def s_ptrans(uid, unit):
                chunks = key_chunks(unit)
                if len(chunks) <= 4:
                    return
                dve.wait_ge(*at(("turned", uid, 1)))
                if before(uid, 2):
                    dve.wait_ge(*at(("pv", before(uid, 2))))
                pt = prob_t[uid[3] % 2]
                whole = [x for x in chunks[4:] if x[1] == P]
                n = len(whole) * P
                half = len(whole) < len(chunks) - 4
                link(V.tensor_copy(pt[:, 512:512 + n], TP[1][:, 0:n]), *([] if half else [("pt", uid, 1)]))
                if half:
                    w = chunks[-1][1]
                    link(V.tensor_copy(pt[0:w, 512 + n:512 + n + P], TP[1][0:w, n:n + P]), ("pt", uid, 1))

            def s_pv(uid, unit):
                _, l, j, i = uid
                hh = unit[0]
                st = stat[:, i % 4, :]
                dve.wait_ge(*at(("softmax_act", uid)))
                if l:
                    link(V.tensor_tensor(st[:, 4:5], st[:, 4:5], st[:, 5:6], ALU.add))
                link(V.reciprocal(st[:, 6:7], st[:, 4:5]))
                dve.wait_ge(*at(("pv", uid)))
                if hh == 0 and before(uid):
                    dve.wait_ge(*at(("ytok_used", before(uid))))
                link(V.tensor_scalar(ytok[:, hh * DH:(hh + 1) * DH], OV[:, 0:DH], st[:, 6:7], None, ALU.mult),
                     ("att_out", uid))

            def s_lin_log(q):
                p, i = q["p"], q["i"]
                dve.wait_ge(*at(("gate_log", p, i)))
                if step_before(q):
                    dve.wait_ge(*at(("scale", *step_before(q))))
                link(V.scalar_tensor_tensor(out=lin(0, "g"), in0=SC[:, 0:2 * P], scalar=0.0, in1=lin(0, "na"),
                                            op0=ALU.min, op1=ALU.subtract), ("g", 0, p, i))

            def s_lin_scale(q):
                l, p, i = q["l"], q["p"], q["i"]
                if i == 0:
                    if step_before(q):
                        dve.wait_ge(*at(("lin_pe", bool(l), 0)))
                    for name in (("kd", "qin") + (("qz",) if l else ())) if p == 0 else ():
                        for odd in range(2):
                            link(V.memset(buf(dict(l=l, i=odd), name), 0.0),
                                 *([("q_zero", 0)] if name == "qz" and odd else []))
                    for d in range(2):
                        link(V.memset(state[d], 0.0), *([("state0", l, p)] if d else []))
                if l and q["wanted"]:
                    dve.wait_ge(*at(("spread", p, i)))
                    link(V.tensor_tensor(by_dir(lin(1, "w", 4)), by_dir(SC[:, 0:4 * P]), over_heads(const("add")),
                                         ALU.add), ("masked", p, i))

            def s_lin_mul(q):
                l, p, i = q["l"], q["p"], q["i"]
                slot = lin_slot(l, p)
                dve.wait_ge(*at(("scale_act", l, p, i)))
                if i >= 2:
                    dve.wait_ge(*at(("update", l, p, i - 2, 1)))
                kd = buf(q, "kd").rearrange("p (c d n) -> p c d n", c=2, d=2)
                for half in range(2):
                    r = slice(half * CHUNK, (half + 1) * CHUNK)
                    if l == 0:
                        link(V.tensor_tensor(kd[r, half, :, :], two(MI[r, 0:2 * P]), two(lin(0, "ekd"))[r, :, :],
                                             ALU.mult))
                        continue
                    for d in range(2):
                        ws = tokc[r, q["t"][d], 1, d * 4 + 2 * p:d * 4 + 2 * p + 2].unsqueeze(2)
                        link(V.tensor_tensor(kd[r, half, d, :].rearrange("p (h n) -> p h n", h=2),
                                             MI[r, d * P:(d + 1) * P].rearrange("p (h n) -> p h n", h=2),
                                             ws.broadcast_to([CHUNK, 2, DH]), ALU.mult),
                             *([("scale_done", l, p, i)] if half and d and not q["wanted"] else []))
                if not q["wanted"]:
                    return
                qin = buf(q, "qin")
                for d in range(2):
                    t = q["t"][d]
                    cs, ds = slice(t * P, (t + 1) * P), slice(d * P, (d + 1) * P)
                    if l == 0:
                        link(V.tensor_tensor(lin(0, "kin")[:, ds], pk(slot)[:, cs], lin(0, "enb")[:, ds], ALU.mult))
                    for h in range(2):
                        r, o = slice(h * DH, (h + 1) * DH), (2 * d + h) * P
                        link(V.tensor_tensor(qin[r, o:o + P], pq(slot)[r, cs], decays(q)[r, ds], ALU.mult),
                             *([("scale_done", l, p, i)] if d and h else []))

            def s_lin_attend(q):
                if not q["wanted"]:
                    return
                l, p, i = q["l"], q["p"], q["i"]
                dve.wait_ge(*at(("attend", l, p, i)))
                if step_before(q, first_wanted(l), 2):
                    dve.wait_ge(*at(("inside", *step_before(q, first_wanted(l), 2))))
                other = by_dir(lin(1, "w", 4)) if l else over_heads(const("mask"))
                link(V.tensor_tensor(by_dir(buf(q, "at")), by_dir(TP[0][:, 0:4 * P]), other, ALU.mult),
                     ("attend_done", l, p, i))

            def s_lin_chunk(q, n):
                l, p, i = q["l"], q["p"], q["i"]
                if i == NT - 1 and n == 1:
                    return
                vw = VW if l else P
                dve.wait_ge(*at(("update", l, p, i, n)))
                for d in range(2):
                    half = n if d == 0 else 1 - n
                    o = d * P + half * CHUNK + (CHUNK - 1 if d == 0 else 0)
                    link(V.scalar_tensor_tensor(out=state[d][:, 0:vw], in0=state[d][:, 0:vw],
                                                scalar=decays(q)[:, o:o + 1], in1=TP[1][:, d * vw:(d + 1) * vw],
                                                op0=ALU.mult, op1=ALU.add), ("state", l, p, i, n, d))

            def s_lin_out(q):
                l, p, i = q["l"], q["p"], q["i"]
                if not q["wanted"]:
                    return
                dve.wait_ge(*at(("lin_o", l, p, i, 1, 1)))
                keys = [("lin_read", l, p, i)] + ([("lin_dve", bool(l), p)] if i == NT - 1 else [])
                if q["second"]:
                    prev = max([y for y in range(i) if y in second_steps(l)], default=None)
                    if prev is not None:
                        dve.wait_ge(*at(("osum_used", l, p, prev)))
                    elif p:
                        dve.wait_ge(*at(("osum_used", l, 0, NT - 1)))
                if l == 0:
                    for d in range(2):
                        o, y = two(out_bank(0, d)), y_block(p, q["t"][d])
                        if q["second"]:
                            link(V.tensor_tensor(two(osum[:, 2 * d * P:2 * (d + 1) * P]), o, y, ALU.add),
                                 *(keys if d else []))
                        else:
                            link(V.tensor_copy(y, o), *(keys if d else []))
                    return
                r = rstat[:, 8:12]
                outs = [out_bank(1, d).rearrange("p (h w) -> p h w", h=2) for d in range(2)]
                for d in range(2):
                    den, em = outs[d][:, :, P], tokc[:, q["t"][d], 2, d * 4 + 2 * p:d * 4 + 2 * p + 2]
                    link(V.scalar_tensor_tensor(out=r[:, 2 * d:2 * d + 2], in0=den, scalar=-1.0, in1=em,
                                                op0=ALU.mult, op1=ALU.max))
                    link(V.tensor_tensor(r[:, 2 * d:2 * d + 2], den, r[:, 2 * d:2 * d + 2], ALU.max))
                link(V.reciprocal(r, r))
                for d in range(2):
                    for h in range(2):
                        kk = keys if d and h else []
                        y, o, ri = y_block(p, q["t"][d])[:, h, :], outs[d][:, h, 0:P], r[:, 2 * d + h:2 * d + h + 1]
                        if q["second"]:
                            link(V.scalar_tensor_tensor(out=osum[:, (2 * d + h) * P:(2 * d + h + 1) * P], in0=o,
                                                        scalar=ri, in1=y, op0=ALU.mult, op1=ALU.add), *kk)
                        else:
                            link(V.tensor_scalar(y, o, ri, None, ALU.mult), *kk)

            def second_steps(l):
                return [1] * (l == 0) + list(range(CT + (NT - CT) // 2, NT))

            def s_lin_norm(q):
                l, p, i = q["l"], q["p"], q["i"]
                dve.wait_ge(*at(("rms", l, p, i)))
                scale = rstat[:, 4:8].unsqueeze(2).broadcast_to([P, 4, P])
                link(V.tensor_tensor(tiles(osum), tiles(osum), scale, ALU.mult), ("lin_y", l, p, i))

            def s_rows():
                dve.wait_ge(*at(("gates_filled",)))
                R = [yT[0:GATE_ROWS, k, :] for k in range(KT)]
                C = [x.rearrange("p (c n) -> p c n", n=CHUNK) for x in R]
                link(V.scalar_tensor_tensor(out=R[2], in0=R[1], scalar=-1.0, in1=R[1], op0=ALU.mult, op1=ALU.min),
                     ("rows_abs",))
                dve.wait_ge(*at(("rows_log",)))
                link(V.scalar_tensor_tensor(out=R[1], in0=R[1], scalar=0.0, in1=R[2], op0=ALU.min, op1=ALU.subtract))

                def running(src, dst, op, by):
                    f, b = slice(0, 32), slice(32, 64)
                    link(V.tensor_tensor(C[dst][f, :, by:], C[src][f, :, by:], C[src][f, :, :CHUNK - by], op))
                    link(V.tensor_copy(C[dst][f, :, :by], C[src][f, :, :by]))
                    link(V.tensor_tensor(C[dst][b, :, :CHUNK - by], C[src][b, :, :CHUNK - by], C[src][b, :, by:], op))
                    link(V.tensor_copy(C[dst][b, :, CHUNK - by:], C[src][b, :, CHUNK - by:]))

                for n in range(6):
                    running(1 + n % 2, 2 - n % 2, ALU.add, 1 << n)
                link(V.tensor_tensor(R[0], R[0], R[1], ALU.subtract))
                for n in range(6):
                    running(0 if n == 0 else 3 - n % 2, 2 + n % 2, ALU.max, 1 << n)
                link(V.memset(rowm[:, :], 0.0))
                for d in range(2):
                    r = slice(32 * d, 32 * d + 32)
                    e = CHUNK - 1 if d == 0 else 0
                    order = [2 * t + (h if d == 0 else 1 - h) for t in scan_order(d) for h in range(2)]
                    for x, y in zip(order, order[1:]):
                        link(V.scalar_tensor_tensor(out=rowm[r, y:y + 1], in0=rowm[r, x:x + 1],
                                                    scalar=C[3][r, x, e:e + 1], in1=C[1][r, x, e:e + 1],
                                                    op0=ALU.max, op1=ALU.add))
                m = rowm[:, :].unsqueeze(2).broadcast_to([GATE_ROWS, T // CHUNK, CHUNK])
                u = rows2[:, 0, :]
                uc = u.rearrange("p (c n) -> p c n", n=CHUNK)
                link(V.tensor_tensor(uc, C[3], m, ALU.max))
                link(V.tensor_scalar(u, u, -1.0, None, ALU.mult))
                link(V.tensor_tensor(rows2[:, 1, :].rearrange("p (c n) -> p c n", n=CHUNK), uc, m, ALU.add))
                for d in range(2):
                    r = slice(32 * d, 32 * d + 32)
                    e = CHUNK - 1 if d == 0 else 0
                    ul = uc[r, :, e:e + 1].broadcast_to([32, T // CHUNK, CHUNK])
                    link(V.tensor_tensor(C[6][r, :, :], C[0][r, :, :], ul, ALU.add))
                link(V.tensor_tensor(R[7], u, R[1], ALU.subtract), ("rows_dve",))

            def s_centre(l, ci, f):
                t0, n = CHUNKS_ALL[ci]
                if f == 0:
                    dve.wait_ge(*at(("sum", l, t0)))
                    link(V.tensor_scalar(mean_neg[:, 0:n], sum_bank(t0)[:, 0:n], -1.0 / D, None, ALU.mult))
                h = hT[:, f, t0:t0 + n]
                link(V.tensor_tensor(h, h, mean_neg[:, 0:n], ALU.add), ("centred", l, ci, f))
                if f >= 2:
                    add_square(l, ci, f - 1)

            def add_square(l, ci, f):
                if tail(l, ci):
                    return
                t0, n = CHUNKS_ALL[ci]
                dve.wait_ge(*at(("square", l, ci, f)))
                link(V.tensor_tensor(total(t0, n), total(t0, n), sq_stage[f % 2][:, 0:n], ALU.add),
                     ("square_used", l, ci, f))

            def s_square_sum(l, ci):
                add_square(l, ci, KT - 1)

            def s_scale(l, ci, f):
                t0, n = CHUNKS_ALL[ci]
                dve.wait_ge(*at(("rstd", l, ci)))
                h = hT[:, f, t0:t0 + n]
                link(V.tensor_tensor(h, h, rstd[:, 0:n], ALU.mult), ("scaled", l, ci, f))

            def s_next(ci, f):
                t0, n = CHUNKS_ALL[ci]
                w = 1 if t0 == 0 else 0
                dve.wait_ge(*at(("x_after", 0, ci, f)))
                link(V.tensor_scalar(hT[:, f, t0:t0 + n], yT[:, f, t0:t0 + n], mods[:, 1, 8 + f, w:w + 1],
                                     mods[:, 1, f, w:w + 1], ALU.mult, ALU.add),
                     *([("h1", ci)] if f == KT - 1 else []))

            part = {"setup": s_setup, "ada": s_ada, "ada_row": s_ada_row, "ada_turn": s_ada_turn,
                    "modulate": s_modulate, "mm": s_mm, "vturn": s_vturn,
                    "rope": s_rope, "softmax": s_softmax, "ptrans": s_ptrans, "pv": s_pv,
                    "lin_log": s_lin_log, "lin_scale": s_lin_scale, "lin_mul": s_lin_mul,
                    "lin_attend": s_lin_attend, "lin_chunk": s_lin_chunk, "lin_out": s_lin_out, "lin_norm": s_lin_norm, "rows": s_rows,
                    "centre": s_centre, "square_sum": s_square_sum, "scale": s_scale, "next": s_next}
            for s in SCHEDULE:
                if s[0] in part:
                    part[s[0]](*s[1:])

        @block.scalar
        def _(act):
            def link(ins, *keys):
                ins.then_inc(*up("scalar_done", *keys))
                act.wait_ge(*c.last("scalar_done"))

            def run(out, in_, func, keys=(), **kw):
                link(nc.scalar.activation(out, in_, func, **kw), *keys)

            def s_setup():
                nc.scalar.preload_act_table_set("natural_log_exp_and_others")
                act.wait_ge(*at(("loaded", "gate_w")))
                run(rstat[:, :], col("cond", 0, 16), ACT.Exp, [("cond_exp",)], scale=-1.0)

            def s_mm(kind, dest, t0, n, u, stage, part):
                if part != 3:
                    return
                ps = PJ[u % 2][:, 0:n]
                if dest == "out":
                    i = RESID_AT[(kind[1], kind[2], t0)]
                    act.wait_ge(*at(("resid", i)))
                    run(x_stage[i % 2][:, 0:n], x_stage[i % 2][:, 0:n], ACT.Copy, [("resid_scaled", i)], scale=ALPHA)
                    return
                act.wait_ge(*at(("proj", u)))
                if stage is not None:
                    if stage >= 2:
                        act.wait_ge(*at(("stage_used", stage - 2)))
                    else:
                        act.wait_ge(*at(("weight_used", "lr")))
                    st = vstage[:, stage % 2, 0:n]
                    if dest == "gate":
                        run(st, ps, ACT.Exp, [("staged", stage)], scale=-1.0)
                    else:
                        run(st, ps, ACT.Copy, [("staged", stage), ("proj_free", u)],
                            scale=QSCALE if dest == "rq" else 1.0)
                elif dest == "lr":
                    act.wait_ge(*at(("lr_ones",)))
                    run(kvT[0:16, t0:t0 + n], PJ[u % 2][0:16, 0:n], ACT.Copy)
                    run(kvT[32:48, t0:t0 + n], PJ[u % 2][32:48, 0:n], ACT.Copy,
                        [("proj_free", u)] + ([("filled_lr",)] if t0 + n == T else []))
                elif dest == "gates":
                    act.wait_ge(*at(("spill", chunk_no(t0))))
                    for k in range(2):
                        r = slice(k * GATE_ROWS, (k + 1) * GATE_ROWS)
                        run(yT[0:GATE_ROWS, k, t0:t0 + n], PJ[u % 2][r, 0:n], ACT.Identity,
                            ([("proj_free", u)] + ([("gates_filled",)] if t0 + n == T else [])) if k else [],
                            bias=cols[r, COLS["gate_b"][0]:COLS["gate_b"][0] + 1])
                elif dest == "kk":
                    act.wait_ge(*at(("lin_pe", False, 1)))
                    run(kvT[:, t0:t0 + n], ps, ACT.Copy, [("proj_free", u)])
                else:
                    slot, prev = pair_slot(kind)
                    for r in readers(prev) if prev and t0 in (0, CTX) else []:
                        act.wait_ge(*at(r))
                    dst = (pq if dest == "q" else pk)(slot)[:, t0:t0 + n]
                    scaled = dest == ("k" if kind[0] == "ml" else "q")
                    run(dst, ps, ACT.Copy, [("proj_free", u)] + ([("filled", *kind)] if t0 + n == T else []),
                        scale=QSCALE if scaled else 1.0)

            def s_vturn(kind, dest, t0, n, u, stage):
                if kind[0] != "ml":
                    return
                slot, prev = pair_slot(kind)
                act.wait_ge(*at(("proj", u)))
                for r in readers(prev) if t0 == 0 else []:
                    act.wait_ge(*at(r))
                nt, t = n // P, t0 // P
                run(pv(slot)[:, t:t + nt, 1 if dest == "v1" else 0, 0:P],
                    PJ[u % 2][:, 0:n].rearrange("p (t n) -> p t n", n=P), ACT.Copy,
                    [("proj_free", u)] + ([("filled", *kind)] if t0 + n == T else []))

            def s_softmax(uid, unit):
                _, l, j, i = uid
                hh, nk = unit[0], unit[3]
                st, pr = stat[:, i % 4, :], prob[i % 2][:, 0:nk + CTX]
                act.wait_ge(*at(("softmax_dve", uid)))
                if l:
                    run(st[:, 5:6], col("sink", j + 4 * hh), ACT.Exp, bias=st[:, 2:3])
                run(pr, pr, ACT.Exp, [("softmax_act", uid)], bias=st[:, 2:3], accum_out=st[:, 4:5])

            def s_ptrans(uid, unit):
                act.wait_ge(*at(("turned", uid, 0)))
                if before(uid, 2):
                    act.wait_ge(*at(("pv", before(uid, 2))))
                n = min(len(key_chunks(unit)), 4) * P
                run(prob_t[uid[3] % 2][:, 0:n], TP[0][:, 0:n], ACT.Copy, [("pt", uid, 0)])

            def s_yout(uid, unit):
                _, l, j, i = uid
                t = unit[1]
                act.wait_ge(*at(("ytok_used", uid)))
                run(yT[:, 4 + j, t * P:(t + 1) * P], MI[:, 0:P], ACT.Copy,
                    [("y_copied", uid)] + ([("y_turned", l, 4 + j)] if i == N_UNITS[l] - 1 else []))

            def s_lin_gate(q):
                p, i, na = q["p"], q["i"], lin(0, "na")
                act.wait_ge(*at(("gate", p, i, 1)))
                if step_before(q):
                    act.wait_ge(*at(("g", *step_before(q))))
                run(na, SC[:, 0:2 * P], ACT.Abs)
                run(na, na, ACT.Exp, scale=-1.0)
                run(na, na, ACT.Ln, [("gate_log", p, i)], bias=col("one", 0))

            def s_lin_scale(q):
                l, p, i = q["l"], q["p"], q["i"]
                act.wait_ge(*at(("scale", l, p, i)))
                if i >= 3:
                    act.wait_ge(*at(("state", l, p, i - 3, 1, 1)))
                elif p:
                    act.wait_ge(*at(("state", l, 0, NT - 1, 0, 1)))
                if l == 0:
                    if step_before(q):
                        act.wait_ge(*at(("scale_done", *step_before(q))))
                    run(lin(0, "ekd"), SC[:, 768:1024], ACT.Exp)
                    run(decays(q), SC[:, 512:768], ACT.Exp)
                    run(lin(0, "enb"), SC[:, 512:768], ACT.Exp, [("scale_act", l, p, i)], scale=-1.0)
                    return
                run(decays(q), MI[:, 256:512], ACT.Copy, [] if q["wanted"] else [("scale_act", l, p, i)])
                if q["wanted"]:
                    act.wait_ge(*at(("masked", p, i)))
                    for d in range(2):
                        for h in range(2):
                            o, hc = (2 * d + h) * P, d * 4 + 2 * p + h
                            w = lin(1, "w", 4)[:, o:o + P]
                            run(w, w, ACT.Exp, [("scale_act", l, p, i)] if d and h else [],
                                bias=tokc[:, q["t"][d], 0, hc:hc + 1])

            def s_lin_out(q):
                if not (q["second"] and q["wanted"]):
                    return
                l, p, i = q["l"], q["p"], q["i"]
                act.wait_ge(*at(("lin_read", l, p, i)))
                for x in range(4):
                    run(squares, osum[:, x * P:(x + 1) * P], ACT.Square, accum_out=rstat[:, x:x + 1])
                run(rstat[:, 0:4], rstat[:, 0:4], ACT.Ln, scale=1.0 / P, bias=col("eps", 1))
                run(rstat[:, 4:8], rstat[:, 0:4], ACT.Exp, [("rms", l, p, i)], scale=-0.5)

            def s_lin_turn(q, u):
                l, p, i = q["l"], q["p"], q["i"]
                act.wait_ge(*at(("proj", u)))
                lo, hi = sorted(q["t"])
                for h in range(2):
                    f = 2 * p + h
                    keys = []
                    if h:
                        keys = [("proj_free", u)]
                        if i == NT - 1:
                            keys += [("y_turned", l, 2 * p), ("y_turned", l, 2 * p + 1), ("lin_act", l, p)]
                    run(yT[:, f, :].rearrange("p (t n) -> p t n", n=P)[:, lo:hi + 1:hi - lo, :],
                        two(PJ[u % 2][:, 2 * h * P:2 * (h + 1) * P]), ACT.Copy, keys, scale=col("norm_g", l * 4 + f))

            def s_rows():
                R = [yT[0:GATE_ROWS, k, :] for k in range(KT)]
                act.wait_ge(*at(("rows_abs",)))
                run(R[2], R[2], ACT.Exp)
                run(R[2], R[2], ACT.Ln, [("rows_log",)], bias=cols[0:GATE_ROWS, COLS["one"][0]:COLS["one"][0] + 1])

            def s_rows_exp():
                R = [yT[0:GATE_ROWS, k, :] for k in range(KT)]
                act.wait_ge(*at(("rows_dve",)))
                run(rows2[:, 1, :], rows2[:, 1, :], ACT.Exp)
                run(R[6], R[6], ACT.Exp)
                run(R[7], R[7], ACT.Exp, [("rows_act",)])

            def s_rows_turn(t, u):
                act.wait_ge(*at(("proj", u)))
                src = PJ[u % 2][:, 0:3 * GATE_ROWS].rearrange("p (i g r) -> p i g r", i=3, g=2)[:, :, :, 0:4]
                for i in range(3):
                    run(tokc[:, t, i, :].rearrange("p (g r) -> p g r", g=2), src[:, i, :, :], ACT.Copy,
                        [("proj_free", u), ("rows_turned", t)] if i == 2 else [])

            def s_centre(l, ci, f):
                t0, n = CHUNKS_ALL[ci]
                act.wait_ge(*at(("centred", l, ci, f)))
                if f >= 3:
                    act.wait_ge(*at(("square_used", l, ci, f - 2)))
                run(sq_stage[f % 2][:, 0:n] if f else total(t0, n), hT[:, f, t0:t0 + n], ACT.Square, [("square", l, ci, f)])

            def s_rstd(l, ci):
                n = CHUNKS_ALL[ci][1]
                act.wait_ge(*at(("square_sum", l, ci)))
                run(rstd[:, 0:n], square_bank(ci)[:, 0:n], ACT.Ln, scale=1.0 / D, bias=col("eps", 0))
                run(rstd[:, 0:n], rstd[:, 0:n], ACT.Exp, [("rstd", l, ci)], scale=-0.5)

            def s_scale(l, ci, f):
                t0, n = CHUNKS_ALL[ci]
                act.wait_ge(*at(("scaled", l, ci, f)))
                run(yT[:, f, t0:t0 + n], hT[:, f, t0:t0 + n], ACT.Identity, [("x_after", l, ci, f)],
                    scale=col("ln_g", l * 8 + f), bias=col("ln_b", l * 8 + f))
                if f % 2:
                    dst, lo = (a["out"], t0 - CTX) if l else (a["x1T"], t0)
                    act.dma_start(dst[f - 1:f + 1, :, lo:lo + n].rearrange("k p n -> p k n"),
                                  yT[:, f - 1:f + 1, t0:t0 + n]).then_inc(
                        *up(f"stored{ci}" if l else f"spilled{ci}",
                            *([("stored" if l else "spill", ci)] if f == KT - 1 else []), by=16))

            part = {"setup": s_setup, "mm": s_mm, "vturn": s_vturn, "softmax": s_softmax, "ptrans": s_ptrans, "yout": s_yout,
                    "lin_gate": s_lin_gate, "lin_scale": s_lin_scale, "lin_out": s_lin_out, "lin_turn": s_lin_turn,
                    "rows": s_rows, "rows_exp": s_rows_exp, "rows_turn": s_rows_turn,
                    "centre": s_centre, "rstd": s_rstd, "scale": s_scale}
            for s in SCHEDULE:
                if s[0] in part:
                    part[s[0]](*s[1:])

        @block.gpsimd
        def _(pool):
            def s_lin_mul(q):
                l, p, i = q["l"], q["p"], q["i"]
                if l == 0 or not q["wanted"]:
                    return
                pool.wait_ge(*at(("q_zero", 0)))
                if p:
                    pool.wait_ge(*at(("lin_pe", True, 0)))
                pool.wait_ge(*at(("filled", "ml", p, "q")))
                if i >= CT + 2:
                    pool.wait_ge(*at(("attend", 1, p, i - 2)))
                for d in range(2):
                    t = q["t"][d]
                    for h in range(2):
                        r, o = slice(h * DH, (h + 1) * DH), (2 * d + h) * P
                        pool.tensor_copy(buf(q, "qz")[r, o:o + P],
                                         pq(lin_slot(1, p))[r, t * P:(t + 1) * P]).then_inc(
                            *up("pool_done", *([("q_padded", p, i)] if d and h else [])))

            def s_mm(kind, dest, t0, n, u, stage, part):
                if dest != "out" or part != 3:
                    return
                l, f = kind[1], kind[2]
                if f == 0:
                    return
                pool.wait_ge(*at(("resid_sum", l, f, t0)))
                if f >= 2:
                    pool.wait_ge(*at(("total", l, f - 1, t0)))
                pool.tensor_tensor(total(t0, n), hT[:, 0, t0:t0 + n] if f == 1 else total(t0, n), hT[:, f, t0:t0 + n],
                                   ALU.add).then_inc(*up("pool_done", ("total", l, f, t0)))

            part = {"lin_mul": s_lin_mul, "mm": s_mm}
            for s in SCHEDULE:
                if s[0] in part:
                    part[s[0]](*s[1:])

    return c.new


def constants():
    i = np.arange(P)
    same = (i[:, None] // CHUNK) == (i[None, :] // CHUNK)
    s, t = i[:, None], i[None, :]
    parts = {
        "ident": np.eye(P), "ones": np.ones((P, P)),
        "tri_f": same * (s <= t) / GLA_TAU, "tri_b": same * (s >= t) / GLA_TAU,
        "stri_f": same * (s > t) / GLA_TAU, "stri_b": same * (s < t) / GLA_TAU,
        "mask": np.concatenate([same * (s <= t), same * (s >= t)], 1),
        "add": np.concatenate([np.where(same & (s <= t), 0.0, NEG), np.where(same & (s >= t), 0.0, NEG)], 1),
        "band": np.concatenate([np.where(t >= s, 0.0, NEG), np.zeros((P, P)), np.where(t <= s, 0.0, NEG)], 1),
    }
    perm = np.zeros((P, P))
    for r in range(P):
        if r % 32 < 16:
            perm[r + 16, r] = -1.0
        else:
            perm[r - 16, r] = 1.0
    parts["perm"] = perm
    out = np.zeros((P, CONST_W), np.float32)
    for name, (o, n) in CONST.items():
        out[:, o:o + n] = parts[name]
    return out


def layer1_tables():
    out = np.zeros((P, TABLES_W), np.float32)
    nf = DH // 4
    freqs = (np.float32(10000.0) ** (-np.arange(nf, dtype=np.float32) / np.float32(nf))).astype(np.float32)
    pos = np.arange(LAT)
    for r in range(P):
        where = (pos // GRID_W if r % DH < DH // 2 else pos % GRID_W).astype(np.float32)
        ang = (where * freqs[r % 16]).astype(np.float32)
        out[r, 0:LAT] = np.cos(ang)
        out[r, LAT:2 * LAT] = np.sin(ang)
    for d in range(2):
        for p in range(2):
            o = SEL_AT + (2 * d + p) * P
            for h in range(2):
                out[32 * d + 2 * p + h, o + h * DH:o + (h + 1) * DH] = 1.0
        for h in range(4):
            o = SEL_AT + (4 + d * 4 + h) * P
            out[32 * d + h, o:o + P] = 1.0
    return out


def weight_tiles(w):
    we, wo_e, wod, wo_o, wa = w["w_in_even"][0], w["w_out_even"][0], w["w_in_odd"][0], w["w_out_odd"][0], w["w_ada"]
    order = np.concatenate([np.r_[j * DH:(j + 1) * DH, (4 + j) * DH:(5 + j) * DH] for j in range(4)])
    wo_o = np.concatenate([wo_o[:512], wo_o[512:][order]])

    def spread(src, starts, width):
        out = np.zeros((D, P), np.float32)
        for to, fr in starts:
            out[:, to:to + width] = src[:, fr:fr + width]
        return out

    def columns(kind):
        k = kind[0]
        if k == "ada":
            return wa[kind[1]][:, kind[2] * P:(kind[2] + 1) * P]
        if k == "lr":
            return spread(we, [(0, 1536), (32, 1552)], 16)
        if k == "gates":
            return spread(wod, [(0, 1536), (64, 1540), (32, 1544), (96, 1548)], 4)
        if k in ("gla", "ml"):
            src, p = (we if k == "gla" else wod), kind[1]
            o = {"q": p * P, "k": 256 + p * P, "v0": 512 + 256 * p, "v1": 640 + 256 * p}[kind[2]]
            return src[:, o:o + P]
        if k == "na":
            o = {"q": 1568, "k": 2080, "v": 2592}[kind[2]] + kind[1] * P
            return we[:, o:o + P]
        if k == "sw":
            if kind[2] == "q":
                return wod[:, 1552 + order[kind[1] * P:(kind[1] + 1) * P]]
            o = {"k": 2064, "v": 2192}[kind[2]]
            return wod[:, o:o + P]
        if k == "gate":
            l, f = kind[1], kind[2]
            if f < 4:
                return (wod if l else we)[:, 1024 + f * P:1024 + (f + 1) * P]
            if l == 0:
                return we[:, 3104 + (f - 4) * P:3104 + (f - 3) * P]
            return wod[:, 2320 + order[(f - 4) * P:(f - 3) * P]]
        return (wo_o if kind[1] else wo_e)[:, kind[2] * P:(kind[2] + 1) * P]

    return np.stack([columns(k).reshape(KT, P, P).transpose(1, 0, 2) for k in PLAN + [("lr",)]])


def bias_tables(rpb):
    q = np.arange(GRID_W)
    start = np.clip(q - 8, 0, GRID_W - 16)
    ok = (q[None, :] >= start[:, None]) & (q[None, :] < start[:, None] + 16)
    dc = np.clip(q[None, :] - q[:, None] + 15, 0, 30)
    out = np.full((8, P, BIAS), NEG, np.float32)
    for half in range(2):
        rows = slice(half * GRID_W, (half + 1) * GRID_W)
        for n, (lo, hi, valid) in enumerate(((1, 15, range(0, 15)), (3, 12, range(3, 11)))):
            for j in range(lo, hi):
                dr = j - half
                if dr not in valid:
                    continue
                o = (FULL_BIAS if n else 0) + (j - lo) * GRID_W
                vals = rpb[:, dr][:, dc]
                out[:, rows, o:o + GRID_W] = np.where(ok[None], vals, np.float32(NEG))
    return out


def layouts(w):
    cols = np.zeros((P, COLS_W), np.float32)

    def put(name, value):
        o, n = COLS[name]
        cols[:, o:o + n] = value

    put("b_ada", w["b_ada"].reshape(2 * 24, P).T)
    put("ln_g", w["ln_g"].reshape(2 * KT, P).T)
    put("ln_b", w["ln_b"].reshape(2 * KT, P).T)
    put("norm_g", np.concatenate([w["gla_norm_g"].reshape(4, P), w["ml_norm_g"].reshape(4, P)]).T)
    put("sink", np.broadcast_to(w["sw_sink"].reshape(1, 8), (P, 8)))
    gb = np.zeros((P, 1), np.float32)
    mb = w["ml_gate_b"].reshape(2, 2, 4)
    for d in range(2):
        gb[32 * d:32 * d + 4, 0] = mb[d, 0]
        gb[64 + 32 * d:64 + 32 * d + 4, 0] = mb[d, 1]
    put("gate_b", gb)
    put("cond", np.stack([w["c"].reshape(KT, P), w["c_ctx"].reshape(KT, P)], 2).transpose(1, 0, 2).reshape(P, 16))
    put("eps", np.array([[LN_EPS, RMS_EPS]], np.float32))
    put("one", 1.0)
    gate_w = np.zeros((P, 512), np.float32)
    for d in range(2):
        gate_w[32 * d:32 * d + 16, d * 256:(d + 1) * 256] = w["gla_gate_w"][0, d]
        gate_w[32 * d + 16, d * 256:(d + 1) * 256] = w["gla_gate_b"][0, d]
    xT = np.concatenate([w["ctx"][0], w["x"][0]]).T.reshape(KT, P, T)
    return {"consts": constants(), "cols": cols, "gate_w": gate_w, "tables": layer1_tables(),
            "bias": bias_tables(w["na_rpb"][0]), "weights": weight_tiles(w), "xT": np.ascontiguousarray(xT)}


def declare(nc, arrays):
    a = {n: nc.dram_tensor(f"in_{n}", v.shape, F32, kind="ExternalInput").ap() for n, v in arrays.items()}
    a["x1T"] = nc.dram_tensor("x1T", (KT, P, T), F32, kind="Internal").ap()
    a["out"] = nc.dram_tensor("out_0", (KT, P, LAT), F32, kind="ExternalOutput").ap()
    return a


def kernel(**inputs):
    from concourse.bacc import Bacc
    from concourse.bass_utils import run_bass_kernel_spmd

    arrays = layouts({k: np.asarray(v) for k, v in inputs.items()})
    counted = None
    for _ in range(2):
        nc = Bacc("TRN2", target_bir_lowering=False, num_devices=1)
        counted = build(nc, declare(nc, arrays), counted)
    r = run_bass_kernel_spmd(nc, [{f"in_{n}": np.ascontiguousarray(v) for n, v in arrays.items()}], core_ids=[0])
    out = r.results[0]["out_0"]
    return np.ascontiguousarray(out.reshape(D, LAT).T).reshape(1, LAT, D)
```
